# Optimizing a Trainium2 kernel written in Bass

```python
import jax, jax.numpy as jnp
from jax import lax
import numpy as np

D_MODEL = 2048
BATCH = 1
SEQ = 256
DEPTH = 1

CHUNK = 64
RET_HEADS = 8
RET_HEAD_DIM = D_MODEL // RET_HEADS
RET_WIDTH = RET_HEADS * RET_HEAD_DIM
SWA_Q_HEADS = 32
SWA_KV_HEADS = 8
SWA_HEAD_DIM = 64
SWA_GROUP = SWA_Q_HEADS // SWA_KV_HEADS
SWA_Q_WIDTH = SWA_Q_HEADS * SWA_HEAD_DIM
SWA_KV_WIDTH = SWA_KV_HEADS * SWA_HEAD_DIM
WINDOW = 128
WINDOW_CHUNKS = -(-WINDOW // CHUNK)
D_FF = -(-(8 * D_MODEL) // (3 * 256)) * 256
ROPE_THETA = 10000.0
EPS = 1e-6
NEG_INF = -1e30
IN_SIZES = [RET_WIDTH, RET_WIDTH, RET_WIDTH, RET_WIDTH,
            SWA_Q_WIDTH, SWA_KV_WIDTH, SWA_KV_WIDTH,
            D_MODEL, D_MODEL]
IN_WIDTH = sum(IN_SIZES)
IN_SPLITS = [int(s) for s in np.cumsum(IN_SIZES)[:-1]]
N_MOD = 6

kernel_name = 'chunk_causal_retention_swa_hybrid_block'

def _rmsnorm(x, gain=None):
    xf = x.astype(jnp.float32)
    y = xf * lax.rsqrt(jnp.mean(xf * xf, axis=-1, keepdims=True) + EPS)
    if gain is not None:
        y = y * gain.astype(jnp.float32)
    return y.astype(x.dtype)

def _rope_tables(positions, head_dim, dtype):
    inv_freq = ROPE_THETA ** (-jnp.arange(0, head_dim, 2, dtype=jnp.float32) / head_dim)
    ang = positions.astype(jnp.float32)[..., None] * inv_freq
    return (jnp.cos(ang)[:, :, None, :].astype(dtype),
            jnp.sin(ang)[:, :, None, :].astype(dtype))

def _rope(x, cos, sin):
    x1, x2 = jnp.split(x, 2, axis=-1)
    return jnp.concatenate([x1 * cos - x2 * sin, x2 * cos + x1 * sin], axis=-1)

def _retention(q, k, v, g, cos, sin):
    B, S, _ = q.shape
    n = S // CHUNK
    dt = q.dtype
    shp = (B, S, RET_HEADS, RET_HEAD_DIM)
    q = _rope(q.reshape(shp), cos, sin)
    k = _rope(k.reshape(shp), cos, sin) * (RET_HEAD_DIM ** -0.5)
    v = v.reshape(shp)
    log_gamma = jnp.log1p(-jnp.exp2(-5.0 - jnp.arange(RET_HEADS, dtype=jnp.float32)))
    idx = jnp.arange(CHUNK, dtype=jnp.float32)
    intra_decay = jnp.exp(log_gamma[:, None, None]
                          * jnp.abs(idx[:, None] - idx[None, :])).astype(dt)
    q_decay = jnp.exp(log_gamma[:, None] * (idx + 1.0)).T.astype(dt)
    k_decay = jnp.exp(log_gamma[:, None] * (CHUNK - 1.0 - idx)).T.astype(dt)
    chunk_decay = jnp.exp(log_gamma * CHUNK).astype(dt)

    cshp = (B, n, CHUNK, RET_HEADS, RET_HEAD_DIM)
    qc, kc, vc = q.reshape(cshp), k.reshape(cshp), v.reshape(cshp)
    scores = jnp.einsum('bnihd,bnjhd->bnhij', qc, kc) * intra_decay
    y_intra = jnp.einsum('bnhij,bnjhe->bnihe', scores, vc)

    def step(state, xs):
        q_n, k_n, v_n = xs
        y = jnp.einsum('bihd,bhde->bihe', q_n * q_decay[:, :, None], state)
        state = (state * chunk_decay[:, None, None]
                 + jnp.einsum('bjhd,bjhe->bhde', k_n * k_decay[:, :, None], v_n))
        return state, y

    state0 = jnp.zeros((B, RET_HEADS, RET_HEAD_DIM, RET_HEAD_DIM), dt)
    xs = (jnp.moveaxis(qc, 1, 0), jnp.moveaxis(kc, 1, 0), jnp.moveaxis(vc, 1, 0))
    _, y_inter = lax.scan(step, state0, xs)
    y = y_intra + jnp.moveaxis(y_inter, 0, 1)
    y = _rmsnorm(y).reshape(B, S, RET_WIDTH)
    return y * jax.nn.silu(g)

def _swa(q, k, v, q_gain, k_gain, sinks, cos, sin):
    B, S, _ = q.shape
    n = S // CHUNK
    q = _rope(_rmsnorm(q.reshape(B, S, SWA_Q_HEADS, SWA_HEAD_DIM), q_gain), cos, sin)
    q = q * (SWA_HEAD_DIM ** -0.5)
    k = _rope(_rmsnorm(k.reshape(B, S, SWA_KV_HEADS, SWA_HEAD_DIM), k_gain), cos, sin)
    v = v.reshape(B, S, SWA_KV_HEADS, SWA_HEAD_DIM)
    qc = q.reshape(B, n, CHUNK, SWA_KV_HEADS, SWA_GROUP, SWA_HEAD_DIM)
    kvshp = (B, n, CHUNK, SWA_KV_HEADS, SWA_HEAD_DIM)

    def band(t):
        t = t.reshape(kvshp)
        pad = jnp.pad(t, ((0, 0), (WINDOW_CHUNKS - 1, 0), (0, 0), (0, 0), (0, 0)))
        return jnp.concatenate([pad[:, w:w + n] for w in range(WINDOW_CHUNKS)], axis=2)

    kb, vb = band(k), band(v)
    key_chunk = (jnp.arange(n)[:, None] - (WINDOW_CHUNKS - 1)
                 + jnp.arange(WINDOW_CHUNKS * CHUNK)[None, :] // CHUNK)
    valid = key_chunk >= 0
    logits = jnp.einsum('bnikgd,bnjkd->bnkgij', qc, kb).astype(jnp.float32)
    logits = jnp.where(valid[None, :, None, None, None, :], logits, NEG_INF)
    sink = jnp.broadcast_to(
        sinks.astype(jnp.float32).reshape(SWA_KV_HEADS, SWA_GROUP, 1, 1),
        logits.shape[:-1] + (1,))
    probs = jax.nn.softmax(jnp.concatenate([logits, sink], axis=-1), axis=-1)[..., :-1]
    out = jnp.einsum('bnkgij,bnjkd->bnikgd', probs.astype(v.dtype), vb)
    return out.reshape(B, S, SWA_Q_WIDTH)

def setup_inputs(seed: int = 0) -> dict:
    key = jax.random.key(seed)
    ks = jax.random.split(key, 20)
    f32 = jnp.float32

    def w(k, shape, fan_in):
        return jax.random.normal(k, shape, f32) * (fan_in ** -0.5)

    def gain(k, shape):
        return 1.0 + 0.02 * jax.random.normal(k, shape, f32)

    offsets = jax.random.randint(ks[2], (BATCH, 1), 0, 4096, dtype=jnp.int32)
    positions = offsets + jnp.arange(SEQ, dtype=jnp.int32)[None, :]
    return {
        'x': jax.random.normal(ks[0], (BATCH, SEQ, D_MODEL), f32),
        'c': jax.random.normal(ks[1], (BATCH, D_MODEL), f32),
        'positions': positions,
        'w_ada': w(ks[3], (DEPTH, D_MODEL, N_MOD * D_MODEL), D_MODEL),
        'b_ada': 0.01 * jax.random.normal(ks[4], (DEPTH, N_MOD * D_MODEL), f32),
        'norm_mix_gain': gain(ks[5], (DEPTH, D_MODEL)),
        'w_in': w(ks[6], (DEPTH, D_MODEL, IN_WIDTH), D_MODEL),
        'q_norm_gain': gain(ks[7], (DEPTH, SWA_HEAD_DIM)),
        'k_norm_gain': gain(ks[8], (DEPTH, SWA_HEAD_DIM)),
        'sinks': 0.5 * jax.random.normal(ks[9], (DEPTH, SWA_Q_HEADS), f32),
        'w_ret_out': w(ks[10], (DEPTH, RET_WIDTH, D_MODEL), RET_WIDTH),
        'w_swa_out': w(ks[11], (DEPTH, SWA_Q_WIDTH, D_MODEL), SWA_Q_WIDTH),
        'w_o': w(ks[12], (DEPTH, D_MODEL, D_MODEL), D_MODEL),
        'norm_ffn_gain': gain(ks[13], (DEPTH, D_MODEL)),
        'w_ffn_in': w(ks[14], (DEPTH, D_MODEL, 2 * D_FF), D_MODEL),
        'w_ffn_out': w(ks[15], (DEPTH, D_FF, D_MODEL), D_FF),
    }

def reference(x, c, positions, w_ada, b_ada, norm_mix_gain, w_in, q_norm_gain,
              k_norm_gain, sinks, w_ret_out, w_swa_out, w_o, norm_ffn_gain,
              w_ffn_in, w_ffn_out):
    dt = x.dtype
    cos_r, sin_r = _rope_tables(positions, RET_HEAD_DIM, dt)
    cos_a, sin_a = _rope_tables(positions, SWA_HEAD_DIM, dt)
    c_act = jax.nn.silu(c)
    for l in range(DEPTH):
        mod = c_act @ w_ada[l] + b_ada[l]
        shift1, scale1, gate1, shift2, scale2, gate2 = [
            m[:, None, :] for m in jnp.split(mod, N_MOD, axis=-1)]

        h = _rmsnorm(x, norm_mix_gain[l]) * (1.0 + scale1) + shift1
        proj = h @ w_in[l]
        r_q, r_k, r_v, r_g, a_q, a_k, a_v, g_a, g_b = jnp.split(proj, IN_SPLITS, axis=-1)
        y_a = _retention(r_q, r_k, r_v, r_g, cos_r, sin_r) @ w_ret_out[l]
        y_b = _swa(a_q, a_k, a_v, q_norm_gain[l], k_norm_gain[l], sinks[l],
                   cos_a, sin_a) @ w_swa_out[l]
        merged = jax.nn.sigmoid(g_a) * y_a + jax.nn.sigmoid(g_b) * y_b
        x = x + gate1 * (merged @ w_o[l])

        h = _rmsnorm(x, norm_ffn_gain[l]) * (1.0 + scale2) + shift2
        f_gate, f_up = jnp.split(h @ w_ffn_in[l], 2, axis=-1)
        x = x + gate2 * ((jax.nn.silu(f_gate) * f_up) @ w_ffn_out[l])
    return x


_drawn_inputs = setup_inputs


def setup_inputs(seed=0):
    import zlib

    import numpy as np

    out = dict(_drawn_inputs(seed))
    spreads = {}
    factors = {'b_ada': 3.346,
     'norm_mix_gain': 5.014,
     'q_norm_gain': 8.0,
     'k_norm_gain': 8.0,
     'sinks': 8.0,
     'norm_ffn_gain': 4.061}
    for name, (base, spread) in spreads.items():
        noise = np.random.default_rng([zlib.crc32(name.encode()), seed]).standard_normal(out[name].shape)
        drawn = base * np.exp(spread * noise) if base else spread * noise
        out[name] = __import__('jax').numpy.asarray(drawn.astype(out[name].dtype))
    for name, factor in factors.items():
        out[name] = (out[name] * factor).astype(out[name].dtype)
    return out
```

```python
from contextlib import ExitStack

import numpy as np

import concourse.bass as bass
from concourse import mybir

F32 = mybir.dt.float32
F32R = mybir.dt.float32r
I32 = mybir.dt.int32
ALU = mybir.AluOpType
ACT = mybir.ActivationFunctionType
AXX = mybir.AxisListType.X

P = 128
D = 2048
SEQ = 256
TT = SEQ // P
KT = D // P
CB = 512
CHUNK = 64
RH, RD = 8, 256
QH, KVH, HD = 32, 8, 64
D_FF = 5632
EPS = 1e-6
THETA = 10000.0
NEG = -1e30
KC = 2
CE = KC * CB
RAW = 8
SPL = 4
AHEAD = 3
NCH = KT // KC

C_RQ, C_RK, C_RV, C_RG = 0, D, 2 * D, 3 * D
C_AQ, C_AK, C_AV = 4 * D, 5 * D, 5 * D + KVH * HD
C_GA, C_GB = 5 * D + 2 * KVH * HD, 6 * D + 2 * KVH * HD
SHIFT1, SCALE1, GATE1, SHIFT2, SCALE2, GATE2 = range(6)

_TP = 2.0 * np.pi
TP1 = float(np.floor(_TP * 2 ** 9) / 2 ** 9)
TP2 = float(np.floor((_TP - TP1) * 2 ** 21) / 2 ** 21)
TP3 = float(np.float32(_TP - TP1 - TP2))
ROUND = float(1.5 * 2 ** 23)
ROUND_HI = ROUND * 2048.0


class At:

    def __init__(self, fixed, loops=()):
        self.fixed, self.loops = fixed, tuple(loops)

    def __add__(self, k):
        return At(self.fixed + k, self.loops)

    def over(self, reg, stride):
        return At(self.fixed, self.loops + ((reg, stride),)) if stride else self

    def value(self, times=1, per=1):
        v = (self.fixed // per) * times
        for reg, stride in self.loops:
            assert stride % per == 0
            v = reg * (stride // per * times) + v
        return v

    def slot(self, size):
        assert all(stride % size == 0 for _, stride in self.loops)
        return self.fixed % size


class Place:

    def __init__(self, n=0, w=0, b=0):
        self.n, self.w, self.b = [x if isinstance(x, At) else At(x) for x in (n, w, b)]

    def over(self, reg, n, w, b):
        return Place(self.n.over(reg, n), self.w.over(reg, w), self.b.over(reg, b))

    def after(self, block):
        return Place(self.n + block.raws, self.w + block.chunks, self.b + 1)


class Block:

    def __init__(self, weights, col, rows=0, chunks=NCH, ada=((), ())):
        self.weights, self.col, self.rows, self.chunks, self.ada = weights, col, rows, chunks, ada
        self.raws = chunks + len(ada[0]) + len(ada[1])

    def offset(self, k):
        return k + (len(self.ada[0]) if k >= 4 else 0)

    def ada_after(self, k):
        return self.ada[0] if k == 3 else self.ada[1] if k == 7 else ()


ADA0 = Place()
N_ADA0 = KT * 4
R_TRIPS, R_N, R_W, R_B = 4, 48, 32, 4
G_TRIPS, G_N, G_W, G_B = 3, 24, 16, 2
F_N, F_W, F_B = 16, 16, 2


def r_blocks(i):
    out = []
    for m, c in enumerate((C_RV, C_RQ, C_RK, C_RG)):
        ada = tuple([(s, SHIFT2 + s, i * 4 + m, h) for h in range(2)] for s in range(2))
        out.append(Block("w_in", (i + c // CB) * CB, ada=ada))
    return out


def gate_ada(acc, section, m):
    if isinstance(m, int) and m == 0:
        return (), tuple([(acc, section, g, h) for g in range(2) for h in range(2)])
    return tuple([(acc, section, m * 2 + g, h) for h in range(2)] for g in range(2))


def ffn_parts():
    n = D_FF // CB
    return [(4 * p, min(4, n - 4 * p)) for p in range(-(-n // 4))]


def sliding_window_fills(first0, first1):
    n, out = [first0, first1], {}

    def use(key, pair):
        n[pair] += 1
        out[key] = n[pair]

    def rest(g):
        for kind in "po":
            for t in range(2):
                use((kind, g, t), t)

    for g in range(4):
        if g:
            rest(g - 1)
        use(("q", g), 0)
        use(("l", g, 0), 0)
        use(("l", g, 1), 1)
    rest(3)
    return out, tuple(n)


def hybrid_block_kernel(nc, x, c, positions, w_ada, b_ada, norm_mix_gain, w_in, q_norm_gain,
                        k_norm_gain, sinks, w_ret_out, w_swa_out, w_o, norm_ffn_gain, w_ffn_in,
                        w_ffn_out, inv_freq, decay, out):
    x_v = x.rearrange("o (t p) n -> p (o t) n", p=P)
    out_v = out.rearrange("o (t p) n -> p (o t) n", p=P)
    rows_v = {
        name: w.rearrange("o (k p) n -> p (o k) n", p=P)
        for name, w in (("w_ada", w_ada), ("w_in", w_in), ("w_ret_out", w_ret_out),
                        ("w_swa_out", w_swa_out), ("w_o", w_o), ("w_ffn_in", w_ffn_in),
                        ("w_ffn_out", w_ffn_out))
    }

    with ExitStack() as ctx:
        def sb(name, shape, dt=F32):
            return ctx.enter_context(nc.sbuf_tensor(name, shape, dt))

        def sem(name):
            return ctx.enter_context(nc.semaphore(name))

        raw = sb("raw", [P, RAW, CE])
        split = sb("split", [P, SPL, 2, KC, CB], F32R)
        res = sb("res", [P, TT, D])
        hT = sb("hT", [P, 2, KT, SEQ], F32R)
        zT = sb("zT", [P, 2, KT, SEQ], F32R)
        acc = sb("acc", [P, 2, D])
        work = sb("work", [P, 4, 2 * CB])
        tmp = sb("tmp", [P, 2, 2 * CB])
        heads = sb("heads", [P, 2 * 2 * CB])
        maskd = sb("maskd", [P, 2, 3 * P])
        decay_sb = sb("decay_sb", [P, 2, 3 * P])
        probs = sb("probs", [P, 2, 2 * CB])
        probsT = sb("probsT", [P, 2, 2 * CB])
        vmix = maskd[:, :, :].rearrange("p h n -> p (h n)")[:, 0:CB]
        cos_r = sb("cos_r", [P, TT, P])
        sin_r = sb("sin_r", [P, TT, P])
        rope_q = sb("rope_q", [P, 2, TT, HD])
        rope_k = sb("rope_k", [P, 2, TT, HD])
        gains = sb("gains", [P, 2, HD])
        ident = sb("ident", [P, P])
        ones = sb("ones", [P, P])
        vecs = sb("vecs", [P, 3, KT])
        modA = sb("modA", [P, KT])
        modB = sb("modB", [P, KT])
        pos_i = sb("pos_i", [P, TT], I32)
        pos_f = sb("pos_f", [P, TT])
        sink_b = sb("sink_b", [P, QH])
        minus_half = sb("minus_half", [P, 16])
        ssum = sb("ssum", [P, 16])
        msq = sb("msq", [P, 16])
        rstd = sb("rstd", [P, 16])
        xsum = sb("xsum", [P, TT, 4])
        smax = sb("smax", [P, 2, 8])
        nmax = sb("nmax", [P, 2, 8])
        dsink = sb("dsink", [P, 2, 8])
        esink = sb("esink", [P, 2, 8])
        rowsum = sb("rowsum", [P, 2, 8])
        den = sb("den", [P, 2, 8])
        rden = sb("rden", [P, 2, 8])

        gemm_ps = ctx.enter_context(nc.psum_tensor("gemm_ps", [P, 2, TT, CB], F32))
        aux_ps = ctx.enter_context(nc.psum_tensor("aux_ps", [P, 2, 2 * CB], F32))

        small_in = [sem(f"small_in{k}") for k in range(3)]
        raw_landed = [sem(f"raw_landed{k}") for k in range(RAW)]
        x_landed = sem("x_landed")
        x_again = [sem(f"x_again{k}") for k in range(2)]
        decay_landed = sem("decay_landed")
        bias_landed = sem("bias_landed")
        stored = sem("stored")
        consts_ready = sem("consts_ready")
        acc_zeroed = sem("acc_zeroed")
        high_ready = sem("high_ready")
        chunk_done = sem("chunk_done")
        w_used = sem("w_used")
        block_taken = [sem(f"block_taken{k}") for k in range(2)]
        aux_filled = [sem(f"aux_filled{k}") for k in range(2)]
        aux_freed = [sem(f"aux_freed{k}") for k in range(2)]
        dve_chain = sem("dve_chain")
        vecs_ready = sem("vecs_ready")
        ss_ready = sem("ss_ready")
        ms_ready = sem("ms_ready")
        rstd_ready = sem("rstd_ready")
        norm_ready = sem("norm_ready")
        hT_high = sem("hT_high")
        hT_ready = sem("hT_ready")
        split_high = sem("split_high")
        tables_ready = sem("tables_ready")
        ang_ready = sem("ang_ready")
        sin_ready = sem("sin_ready")
        roped = sem("roped")
        merged = sem("merged")
        vmix_ready = sem("vmix_ready")
        q_squared = sem("q_squared")
        q_ready = sem("q_ready")
        max_ready = sem("max_ready")
        exp_ready = sem("exp_ready")
        rden_ready = sem("rden_ready")
        probs_ready = sem("probs_ready")
        o_high = sem("o_high")
        x1_ready = sem("x1_ready")
        out_ready = sem("out_ready")

        R0 = Place(N_ADA0)
        G0 = Place(N_ADA0 + R_TRIPS * R_N, R_TRIPS * R_W, R_TRIPS * R_B)

        class Gate:

            def __init__(self, start, col, w_out, a, section):
                self.start, self.col, self.w_out, self.a, self.section = start, col, w_out, a, section
                self.first = Block("w_in", col, ada=gate_ada(a, section, 0))
                self.loop = start.after(self.first)
                self.last = Block(w_out, 3 * CB, ada=gate_ada(a, section, 7))
                n = self.loop
                self.last_at = Place(n.n + G_TRIPS * G_N, n.w + G_TRIPS * G_W, n.b + G_TRIPS * G_B)
                self.end = self.last_at.after(self.last)

            def trip(self, j):
                return [Block(self.w_out, j * CB, ada=gate_ada(self.a, self.section, j * 2 + 1)),
                        Block("w_in", j * CB + (self.col + CB), ada=gate_ada(self.a, self.section, j * 2 + 2))]

        GA = Gate(G0, C_GA, "w_ret_out", 0, GATE1)
        s_blocks = [Block("w_in", C_AV), Block("w_in", C_AK)] + [
            Block("w_in", C_AQ + g * CB) for g in range(4)]
        s_at = [GA.end]
        for blk in s_blocks:
            s_at.append(s_at[-1].after(blk))

        class LateGate:

            TRIPS = 2

            def __init__(self, start, col, w_out, a, section):
                self.col, self.w_out, self.a, self.section = col, w_out, a, section
                self.firsts = [Block("w_in", col + m * CB, ada=self.ada(m)) for m in range(2)]
                self.lasts = [Block(w_out, m * CB, ada=self.ada(4 + m)) for m in (2, 3)]
                self.first_at = [start, start.after(self.firsts[0])]
                self.loop = n = self.first_at[1].after(self.firsts[1])
                t = self.TRIPS
                self.last_at = [Place(n.n + t * G_N, n.w + t * G_W, n.b + t * G_B)]
                self.last_at.append(self.last_at[0].after(self.lasts[0]))
                self.end = self.last_at[1].after(self.lasts[1])

            def ada(self, m):
                return tuple([(self.a, self.section, m * 2 + g, h) for h in range(2)] for g in range(2))

            def trip(self, j):
                return [Block(self.w_out, j * CB, ada=self.ada(j * 2 + 2)),
                        Block("w_in", j * CB + (self.col + 2 * CB), ada=self.ada(j * 2 + 3))]

        GB = LateGate(s_at[-1], C_GB, "w_swa_out", 1, GATE2)
        o_blocks = [Block("w_o", j * CB) for j in range(4)]
        o_at = [GB.end]
        for blk in o_blocks:
            o_at.append(o_at[-1].after(blk))

        class Part:

            def __init__(self, start, first, pairs):
                self.start, self.first, self.pairs = start, first, pairs
                self.loop = start.after(Block("w_ffn_in", 0)).after(Block("w_ffn_in", 0))
                k = pairs - 1
                self.out_at = [Place(self.loop.n + k * F_N, self.loop.w + k * F_W, self.loop.b + k * F_B)]
                self.outs = [Block("w_ffn_out", j * CB, rows=first * 4, chunks=pairs * 4 // KC) for j in range(4)]
                for blk in self.outs:
                    self.out_at.append(self.out_at[-1].after(blk))

            def pair(self, j):
                col = (self.first + j) * CB if isinstance(j, int) else j * CB + self.first * CB
                return [Block("w_ffn_in", col), Block("w_ffn_in", col + D_FF)]

        parts, at = [], o_at[-1]
        for first, pairs in ffn_parts():
            parts.append(Part(at, first, pairs))
            at = parts[-1].out_at[-1]

        def shifted(loop, j):
            return Place(*[At(v.fixed - s, v.loops).over(j, s)
                           for v, s in ((loop.n, F_N), (loop.w, F_W), (loop.b, F_B))])

        def taken(b):
            return (b + 4).value(1, 2)

        AUX_R = (3, 3)
        AUX_GA = (AUX_R[0] + 8, AUX_R[1] + 8)
        AUX_S = (AUX_GA[0] + 2, AUX_GA[1] + 3)
        SW_FILL, AUX_GB = sliding_window_fills(AUX_S[0] + 1, AUX_S[1] + 1)
        AUX_O = (AUX_GB[0] + 2, AUX_GB[1] + 1)
        AUX_F = (AUX_O[0] + 4, AUX_O[1] + 5)

        def wslot(k):
            return work[:, k, :].rearrange("p (t n) -> p t n", t=TT)

        block = ctx.enter_context(nc.Block())

        @block.sync
        def _(sp):
            vrows = tmp[:, 0, 0:P]
            sp.wait_ge(consts_ready, 3)
            for k, v in enumerate((c, norm_mix_gain, norm_ffn_gain)):
                sp.dma_start(tmp[16 * k:16 * k + 16, 0, 0:P],
                             v.rearrange("o (k p) -> (o k) p", p=P)).then_inc(small_in[0], 16)
            with nc.allow_non_contiguous_dma(reason="256 positions"):
                sp.dma_start(pos_i[:, :], positions.rearrange("o (t p) -> p (o t)", p=P)).then_inc(small_in[1], 16)
            sp.dma_start(tmp[:, 1, 0:P], inv_freq.to_broadcast([P, P])).then_inc(small_in[1], 16)
            sp.dma_start(gains[:, 0, :], q_norm_gain.to_broadcast([P, HD])).then_inc(small_in[2], 16)
            sp.dma_start(gains[:, 1, :], k_norm_gain.to_broadcast([P, HD])).then_inc(small_in[2], 16)
            sp.dma_start(sink_b[:, :], sinks.to_broadcast([P, QH])).then_inc(small_in[2], 16)
            sp.dma_start(res[:, :, :], x_v).then_inc(x_landed, 16)

            def load(n, src):
                if n.loops or n.fixed >= RAW:
                    sp.wait_ge(chunk_done, (n + (1 - RAW)).value())
                s = n.slot(RAW)
                dst = raw[:, s, :].rearrange("p (k n) -> p k n", k=src.shape[1])
                sp.dma_start(dst, src).then_inc(raw_landed[s], 16)

            def load_ada(n, section, kt, half):
                load(n, rows_v["w_ada"][:, bass.ds(kt, 1), section * D + half * CE:section * D + (half + 1) * CE])

            def load_block(at, blk):
                r = 0
                for k in range(blk.chunks):
                    kt = blk.rows + KC * k
                    load(at.n + r, rows_v[blk.weights][:, kt:kt + KC, bass.ds(blk.col, CB)])
                    r += 1
                    for _, section, akt, half in blk.ada_after(k):
                        load_ada(at.n + r, section, akt, half)
                        r += 1

            def load_all(at, blks):
                for blk in blks:
                    load_block(at, blk)
                    at = at.after(blk)

            def load_mod(k, kt):
                sp.dma_start(raw[:, k, :].rearrange("p (k n) -> p k n", k=1),
                             rows_v["w_ada"][:, bass.ds(kt, 1), k % 4 * CE:(k % 4 + 1) * CE]).then_inc(raw_landed[k], 16)

            for k in range(RAW):
                load_mod(k, k // 4)
            with sp.Fori(1, N_ADA0 // RAW) as i:
                kts = [i * 2, i * 2 + 1]
                for k in range(RAW):
                    sp.wait_ge(chunk_done, i * RAW + (k + 1 - RAW))
                    load_mod(k, kts[k // 4])
            with sp.Fori(0, R_TRIPS) as i:
                at, blks = R0.over(i, R_N, R_W, R_B), r_blocks(i)
                load_block(at, blks[0])
                head = i * 2
                sp.wait_ge(aux_freed[0], i * 2 + AUX_R[0])
                sp.dma_start(decay_sb[:, :, :], decay[:, bass.ds(head, 2), :]).then_inc(decay_landed, 16)
                load_all(at.after(blks[0]), blks[1:])

            def load_gate(G):
                load_block(G.start, G.first)
                with sp.Fori(0, G_TRIPS) as j:
                    load_all(G.loop.over(j, G_N, G_W, G_B), G.trip(j))
                load_block(G.last_at, G.last)

            load_gate(GA)
            for at_, blk in zip(s_at, s_blocks):
                load_block(at_, blk)
            load_all(GB.first_at[0], GB.firsts)
            with sp.Fori(0, GB.TRIPS) as j:
                load_all(GB.loop.over(j, G_N, G_W, G_B), GB.trip(j))
            load_all(GB.last_at[0], GB.lasts)
            for j, (at_, blk) in enumerate(zip(o_at, o_blocks)):
                load_block(at_, blk)
                if j == 0:
                    sp.wait_ge(merged, 4)
                if j >= 2:
                    sp.wait_ge(x1_ready, j - 1)
                sp.dma_start(work[:, j % 2, :].rearrange("p (t n) -> p t n", t=TT),
                             x_v[:, :, j * CB:(j + 1) * CB]).then_inc(x_again[j % 2], 16)
            for part in parts:
                load_all(part.start, part.pair(0))
                with sp.Fori(1, part.pairs) as j:
                    load_all(shifted(part.loop, j), part.pair(j))
                for at_, blk in zip(part.out_at, part.outs):
                    load_block(at_, blk)
            for j in range(4):
                sp.wait_ge(out_ready, j + 1)
                sp.dma_start(out_v[:, :, j * CB:(j + 1) * CB], res[:, :, j * CB:(j + 1) * CB]).then_inc(stored, 16)
            sp.wait_ge(stored, 64)

        @block.gpsimd
        def _(pool):
            nc.gpsimd.memset(ident[:, :], 0.0).then_inc(consts_ready, 1)
            nc.gpsimd.memset(ones[:, :], 1.0).then_inc(consts_ready, 1)
            nc.gpsimd.memset(tmp[:, 0, 0:P], 0.0).then_inc(consts_ready, 1)
            pool.wait_ge(consts_ready, 1)
            nc.gpsimd.affine_select(out=ident[:, :], in_=ident[:, :], compare_op=ALU.not_equal, fill=1.0,
                                    base=0, pattern=[[-1, P]], channel_multiplier=1).then_inc(consts_ready, 1)
            nc.gpsimd.memset(minus_half[:, :], -0.5).then_inc(consts_ready, 1)
            zeroed = [0]

            def start_acc(a, section):
                nc.gpsimd.memset(acc[:, a, :], 0.0).then_inc(acc_zeroed, 1)
                zeroed[0] += 1
                pool.wait_ge(acc_zeroed, zeroed[0])
                pool.dma_start(acc[0:1, a, :], b_ada[:, section * D:(section + 1) * D]).then_inc(bias_landed, 16)

            def rsqrt(k, cols):
                pool.wait_ge(ms_ready, k)
                nc.gpsimd.tensor_tensor(rstd[:, 0:cols], msq[:, 0:cols], minus_half[:, 0:cols],
                                        ALU.pow).then_inc(rstd_ready, 1)

            start_acc(0, SHIFT1)
            start_acc(1, SCALE1)
            pool.wait_ge(consts_ready, 5)
            rsqrt(1, TT)
            pool.wait_ge(aux_filled[1], 1)
            start_acc(0, SHIFT2)
            start_acc(1, SCALE2)
            with pool.Fori(0, R_TRIPS) as i:
                rsqrt(i + 2, 4)
            pool.wait_ge(aux_filled[1], AUX_GA[1] + 1)
            start_acc(0, GATE1)
            start_acc(1, GATE2)
            pool.wait_ge(block_taken[s_at[0].b.slot(2)], taken(s_at[0].b))
            v = work[:, 3, :].rearrange("p (t n) -> p t n", t=TT)
            nc.gpsimd.tensor_copy(vmix[0:CHUNK, :], v[0:CHUNK, 1, :]).then_inc(vmix_ready, 1)
            pool.wait_ge(vmix_ready, 1)
            nc.gpsimd.tensor_copy(vmix[CHUNK:P, :], v[CHUNK:P, 0, :]).then_inc(vmix_ready, 1)
            pool.wait_ge(vmix_ready, 2)

            def square(k):
                b = s_at[1 + k].b
                pool.wait_ge(block_taken[b.slot(2)], taken(b))
                nc.gpsimd.tensor_tensor(tmp[:, 1, :], work[:, 0, :], work[:, 0, :], ALU.mult).then_inc(q_squared, 1)

            def normalise(k):
                pool.wait_ge(rden_ready, k + 1)
                p3 = probs[:, k % 2, :].rearrange("p (h j) -> p h j", h=8)
                nc.gpsimd.tensor_tensor(p3, p3, rden[:, k % 2, :].unsqueeze(2).to_broadcast([P, 8, P]),
                                        ALU.mult).then_inc(probs_ready, 1)

            square(0)
            rsqrt(R_TRIPS + 2, 16)
            square(1)
            rsqrt(R_TRIPS + 3, 16)
            for g in range(4):
                if g < 3:
                    square(g + 2)
                normalise(2 * g)
                if g < 3:
                    rsqrt(R_TRIPS + 4 + g, 16)
                normalise(2 * g + 1)
            rsqrt(R_TRIPS + 7, TT)

        @block.scalar
        def _(act):
            def prep(at, blk, k):
                n, w = at.n + blk.offset(k), at.w + k
                s, r = w.slot(SPL), n.slot(RAW)
                act.wait_ge(raw_landed[r], (n + RAW).value(16, RAW))
                if w.loops or w.fixed >= SPL:
                    act.wait_ge(w_used, (w + (2 - SPL)).value())
                nc.scalar.activation(split[:, s, 0, :, :], raw[:, r, :].rearrange("p (k n) -> p k n", k=KC),
                                     ACT.Copy).then_inc(high_ready, 1)

            def step(at, blk, hooks=None, nxt=True):
                hooks = hooks or {}
                for k in range(AHEAD, blk.chunks + (AHEAD if nxt else 0)):
                    if k in hooks:
                        hooks[k]()
                    if k < blk.chunks:
                        prep(at, blk, k)
                    else:
                        prep(at.after(blk), FIRST, k - blk.chunks)

            def take(at, blk, out, func):
                act.wait_ge(w_used, (at.w + (blk.chunks + 1)).value())
                q = at.b.slot(2)
                return nc.scalar.activation(out, gemm_ps[:, q, :, :], func).then_inc(block_taken[q], 1)

            act.wait_ge(aux_filled[0], 1)
            nc.scalar.activation(vecs[:, 0, :], aux_ps[:, 0, 0:KT], ACT.Silu).then_inc(vecs_ready, 1)
            act.wait_ge(vecs_ready, 1)
            nc.scalar.activation(vecs[:, 1:3, :], aux_ps[:, 0, KT:3 * KT].rearrange("p (a b) -> p a b", a=2),
                                 ACT.Copy).then_inc(aux_freed[0], 1)
            act.wait_ge(ang_ready, 1)
            nc.scalar.activation(sin_r[:, :, :], work[:, 0, 0:SEQ].rearrange("p (t n) -> p t n", t=TT),
                                 ACT.Sin).then_inc(sin_ready, 1)
            nc.scalar.activation(work[:, 1, 0:SEQ], work[:, 0, 0:SEQ], ACT.Sin, scale=0.5).then_inc(sin_ready, 1)
            act.wait_ge(x_landed, 16)
            for t in range(TT):
                nc.scalar.activation(gemm_ps[:, :, :, :].rearrange("p a b n -> p (a b n)"), res[:, t, :],
                                     ACT.Square, accum_out=ssum[:, t:t + 1]).then_inc(block_taken[t], 1)
                act.wait_ge(block_taken[t], 1)
            nc.scalar.activation(xsum[:, :, 0], ssum[:, 0:TT], ACT.Copy).then_inc(ss_ready, 1)

            def high_h(k, fills):
                act.wait_ge(aux_freed[k % 2], fills[k % 4])
                g = k % 4
                nc.scalar.activation(hT[:, 0, 4 * g:4 * g + 4, :],
                                     tmp[:, k % 2, :].rearrange("p (k n) -> p k n", k=4),
                                     ACT.Copy).then_inc(hT_high, 1)

            FIRST = Block("", 0)
            for k in range(AHEAD):
                prep(R0, FIRST, k)
            for g in range(4):
                high_h(g, [2, 2, 3, 3])

            def high_split(dst, pair, filled, kt):
                act.wait_ge(aux_filled[pair], filled)
                nc.scalar.activation(dst[:, 0, bass.ds(kt, 4), :],
                                     aux_ps[:, pair, :].rearrange("p (k n) -> p k n", k=4),
                                     ACT.Copy).then_inc(split_high, 1)

            with act.Fori(0, R_TRIPS) as i:
                at = R0.over(i, R_N, R_W, R_B)
                bv, bq, bk, bg = r_blocks(i)
                a0, a1 = AUX_R

                def filled(pair, k):
                    return i * 2 + ((a0, a1)[pair] + k + 1)

                step(at, bv)
                act.wait_ge(aux_filled[1], filled(1, -1))
                take(at, bv, wslot(2), ACT.Copy)
                at = at.after(bv)
                step(at, bq)
                act.wait_ge(aux_filled[0], filled(0, -2))
                take(at, bq, wslot(0), ACT.Copy)
                at = at.after(bq)

                def take_heads(pair, dst, k):
                    act.wait_ge(aux_filled[pair], filled(pair, 0))
                    nc.scalar.activation(heads[:, dst * 2 * CB:(dst + 1) * 2 * CB], aux_ps[:, pair, :],
                                         ACT.Copy).then_inc(aux_freed[pair], 1)

                step(at, bk, {10: lambda: take_heads(0, 0, 0)})
                act.wait_ge(aux_filled[1], filled(1, -2))
                take(at, bk, wslot(1), ACT.Copy)
                at = at.after(bk)
                step(at, bg, {7: lambda: take_heads(1, 1, 0)})
                act.wait_ge(aux_freed[1], i * 2 + a1)
                take(at, bg, wslot(3), ACT.Silu)
                act.wait_ge(aux_filled[1], filled(1, 1))
                for t in range(TT):
                    for hd in range(2):
                        ins = nc.scalar.activation(probs[:, hd, t * RD:(t + 1) * RD],
                                                   aux_ps[:, 1, t * CB + hd * RD:t * CB + (hd + 1) * RD],
                                                   ACT.Square, accum_out=ssum[:, 2 * t + hd:2 * t + hd + 1])
                ins.then_inc(ss_ready, 1)

            def gates(G, first_hooks):
                step(G.start, G.first, first_hooks)
                take(G.start, G.first, wslot(0), ACT.Sigmoid)
                with act.Fori(0, G_TRIPS) as j:
                    at = G.loop.over(j, G_N, G_W, G_B)
                    bo, bgt = G.trip(j)
                    bo_at = at
                    step(at, bo)
                    at = at.after(bo)
                    step(at, bgt)
                    act.wait_ge(block_taken[bo_at.b.slot(2)], taken(bo_at.b))
                    take(at, bgt, wslot(0), ACT.Sigmoid)

            def take_gate_row(a, h, pair, filled):
                act.wait_ge(aux_filled[pair], filled)
                nc.scalar.activation(acc[:, a, h * CE:(h + 1) * CE], aux_ps[:, pair, :],
                                     ACT.Copy).then_inc(aux_freed[pair], 1)

            a0, a1 = AUX_GA
            gates(GA, {6: lambda: high_split(zT, 0, a0 + 1, 0),
                       7: lambda: high_split(zT, 1, a1 + 2, 4),
                       9: lambda: high_split(zT, 0, a0 + 2, 8),
                       10: lambda: high_split(zT, 1, a1 + 3, 12)})
            step(GA.last_at, GA.last)

            a0, a1 = AUX_S
            qfill = [a0 + 1, a1 + 1]

            def q_take(g):
                act.wait_ge(q_ready, g + 1)
                take(s_at[2 + g], s_blocks[2 + g], wslot(0), ACT.Copy)

            def take_kT(p):
                act.wait_ge(aux_filled[p], (a0, a1)[p] + 1)
                nc.scalar.activation(heads[:, p * 2 * CB:(p + 1) * 2 * CB], aux_ps[:, p, :],
                                     ACT.Copy).then_inc(aux_freed[p], 1)

            def take_qT(g):
                act.wait_ge(aux_filled[0], SW_FILL["q", g])
                nc.scalar.activation(work[:, 2, :], aux_ps[:, 0, :],
                                     ACT.Copy).then_inc(aux_freed[0], 1)

            def exps(g, t):
                act.wait_ge(max_ready, 2 * g + t + 1)
                if g:
                    act.wait_ge(aux_filled[t], SW_FILL["p", g - 1, t])
                for h in range(8):
                    ins = nc.scalar.activation(probs[:, t, h * P:(h + 1) * P], aux_ps[:, t, h * P:(h + 1) * P],
                                               ACT.Exp, bias=nmax[:, t, h:h + 1],
                                               accum_out=rowsum[:, t, h:h + 1])
                ins.then_inc(aux_freed[t], 1)
                nc.scalar.activation(esink[:, t, :], dsink[:, t, :], ACT.Exp).then_inc(exp_ready, 1)

            def take_pT(g, t):
                act.wait_ge(aux_filled[t], SW_FILL["p", g, t])
                if g:
                    act.wait_ge(o_high, 2 * g)
                nc.scalar.activation(probsT[:, t, :], aux_ps[:, t, :],
                                     ACT.Copy).then_inc(aux_freed[t], 1)

            def o_take(g, t):
                act.wait_ge(aux_filled[t], SW_FILL["o", g, t])
                nc.scalar.activation(zT[:, 0, 4 * g:4 * g + 4, t * P:(t + 1) * P],
                                     aux_ps[:, t, 0:CB].rearrange("p (k n) -> p k n", k=4),
                                     ACT.Copy).then_inc(o_high, 1)

            def take_pTs(g):
                take_pT(g, 0)
                take_pT(g, 1)

            def o_takes(g):
                o_take(g, 0)
                o_take(g, 1)

            step(s_at[0], s_blocks[0])
            act.wait_ge(aux_freed[1], AUX_GA[1])
            take(s_at[0], s_blocks[0], wslot(3), ACT.Copy)
            step(s_at[1], s_blocks[1])
            q = GA.last_at.b.slot(2)
            act.wait_ge(block_taken[q], taken(GA.last_at.b))
            take(s_at[1], s_blocks[1], wslot(0), ACT.Copy)
            step(s_at[2], s_blocks[2])
            take_kT(0)
            take_kT(1)
            q_take(0)
            for g in range(3):
                hooks = {}
                if g:
                    hooks = {4: lambda: exps(g - 1, 1), 8: lambda: take_pT(g - 1, 0),
                             9: lambda: take_pT(g - 1, 1), 10: lambda: o_takes(g - 1)}
                step(s_at[3 + g], s_blocks[3 + g], hooks)
                take_qT(g)
                q_take(g + 1)
                exps(g, 0)
            step(GB.first_at[0], GB.firsts[0],
                 {4: lambda: exps(2, 1), 8: lambda: take_pT(2, 0), 9: lambda: take_pT(2, 1),
                  10: lambda: o_takes(2)})
            take_qT(3)
            exps(3, 0)

            def first_gate():
                act.wait_ge(q_ready, 5)
                take(GB.first_at[0], GB.firsts[0], wslot(0), ACT.Sigmoid)

            step(GB.first_at[1], GB.firsts[1],
                 {4: lambda: exps(3, 1), 6: first_gate, 8: lambda: take_pT(3, 0), 9: lambda: take_pT(3, 1),
                  10: lambda: o_takes(3)})
            take(GB.first_at[1], GB.firsts[1], wslot(1), ACT.Sigmoid)
            with act.Fori(0, GB.TRIPS) as j:
                at = GB.loop.over(j, G_N, G_W, G_B)
                bo, bgt = GB.trip(j)
                step(at, bo)
                at = at.after(bo)
                step(at, bgt)
                act.wait_ge(merged, j + 1)
                take(at, bgt, work[:, bass.ds(j, 1), :].rearrange("p a (t n) -> p (a t) n", t=TT), ACT.Sigmoid)
            step(GB.last_at[0], GB.lasts[0])
            g0, g1 = AUX_GB
            step(GB.last_at[1], GB.lasts[1], {6: lambda: high_split(hT, 0, g0 + 1, 0),
                                              8: lambda: high_split(hT, 1, g1 + 1, 4),
                                              10: lambda: high_split(hT, 0, g0 + 2, 8)})
            o0, o1 = AUX_O
            step(o_at[0], o_blocks[0], {6: lambda: high_split(hT, 1, o1 + 1, 12),
                                        8: lambda: take_gate_row(0, 0, 0, o0 + 1),
                                        9: lambda: take_gate_row(0, 1, 1, o1 + 2)})
            for j in range(4):
                if j:
                    hooks = {}
                    if j == 1:
                        hooks = {8: lambda: take_gate_row(1, 0, 0, o0 + 2),
                                 9: lambda: take_gate_row(1, 1, 1, o1 + 3)}
                    step(o_at[j], o_blocks[j], hooks)
                act.wait_ge(x1_ready, j + 1)
                for t in range(TT):
                    ins = nc.scalar.activation(probs[:, t, 0:CB], res[:, t, j * CB:(j + 1) * CB], ACT.Square,
                                               accum_out=xsum[:, t, j:j + 1])
                ins.then_inc(ss_ready, 1)
            h2_fills = [AUX_F[0] - 1, AUX_F[1] - 1, AUX_F[0], AUX_F[1]]
            high_h(4, h2_fills)
            high_h(5, h2_fills)

            for p, part in enumerate(parts):
                def ffn_pair(at, j, k, T=None):
                    gate, up = part.pair(j)
                    hooks = {8: T} if T else {}
                    if isinstance(k, int) and k == 0:
                        hooks = {4: lambda: high_h(6, h2_fills), 5: lambda: high_h(7, h2_fills)}
                    step(at, gate, hooks)
                    act.wait_ge(block_taken[1], taken(at.b + -1))
                    take(at, gate, wslot(0), ACT.Silu)
                    at = at.after(gate)
                    step(at, up)

                f1 = AUX_F[1] + 4 * p
                ffn_pair(part.start, 0, part.first)
                with act.Fori(1, part.pairs) as j:
                    ffn_pair(shifted(part.loop, j), j, j + part.first,
                             lambda: high_split(zT, 1, j + f1, j * 4 - 4))
                for m, (at_, blk) in enumerate(zip(part.out_at, part.outs)):
                    last = p == len(parts) - 1 and m == 3
                    hooks = {5: lambda: high_split(zT, 1, f1 + part.pairs, 4 * part.pairs - 4)} if m == 0 else {}
                    step(at_, blk, hooks, nxt=not last)

        @block.vector
        def _(dve):
            chain = [At(0)]

            def link(ins):
                ins.then_inc(dve_chain, 1)
                chain[0] = chain[0] + 1
                return ins

            def settle():
                dve.wait_ge(dve_chain, chain[0].value())

            def low(at, blk, k):
                n, w = at.n + blk.offset(k), at.w + k
                s, r = w.slot(SPL), n.slot(RAW)
                dve.wait_ge(high_ready, (w + 1).value())
                nc.vector.tensor_tensor(split[:, s, 1, :, :], raw[:, r, :].rearrange("p (k n) -> p k n", k=KC),
                                        split[:, s, 0, :, :].bitcast(F32), ALU.subtract).then_inc(chunk_done, 1)

            def ada(n, a, kt, half):
                r = n.slot(RAW)
                dve.wait_ge(raw_landed[r], (n + RAW).value(16, RAW))
                dve.wait_ge(chunk_done, (n + (-1)).value())
                dst = acc[:, a, half * CE:(half + 1) * CE]
                nc.vector.scalar_tensor_tensor(out=dst, in0=raw[:, r, :], scalar=vecs[:, 0, bass.ds(kt, 1)],
                                               in1=dst, op0=ALU.mult, op1=ALU.add).then_inc(chunk_done, 1)

            def step(at, blk, hooks=None, nxt=True):
                hooks = hooks or {}
                for k in range(AHEAD, blk.chunks + (AHEAD if nxt else 0)):
                    if k in hooks:
                        hooks[k]()
                    if k >= blk.chunks:
                        low(at.after(blk), FIRST, k - blk.chunks)
                        continue
                    low(at, blk, k)
                    for m, (a, _, kt, half) in enumerate(blk.ada_after(k)):
                        ada(at.n + (blk.offset(k) + 1 + m), a, kt, half)

            FIRST = Block("", 0)

            invf = tmp[:, 1, 0:P]
            dve.wait_ge(small_in[1], 32)
            link(nc.vector.tensor_copy(pos_f[:, :], pos_i[:, :]))
            settle()
            ang = work[:, 0, 0:SEQ]
            turns, hi, lo_ = work[:, 1, 0:SEQ], work[:, 2, 0:SEQ], work[:, 3, 0:SEQ]
            for t in range(TT):
                link(nc.vector.tensor_scalar(ang[:, t * P:(t + 1) * P], invf, pos_f[:, t:t + 1], None, ALU.mult))
            settle()
            link(nc.vector.tensor_scalar(turns, ang, 1.0 / _TP, ROUND, ALU.mult, ALU.add))
            settle()
            link(nc.vector.tensor_scalar(turns, turns, ROUND, None, ALU.subtract))
            settle()
            link(nc.vector.tensor_scalar(hi, turns, ROUND_HI, None, ALU.add))
            settle()
            link(nc.vector.tensor_scalar(hi, hi, ROUND_HI, None, ALU.subtract))
            settle()
            link(nc.vector.tensor_tensor(lo_, turns, hi, ALU.subtract))
            settle()
            for mult, by in ((hi, TP1), (lo_, TP1), (hi, TP2), (lo_, TP2), (turns, TP3)):
                link(nc.vector.scalar_tensor_tensor(out=ang, in0=mult, scalar=-by, in1=ang,
                                                    op0=ALU.mult, op1=ALU.add))
                settle()
            PI = 3.1415925
            nc.vector.tensor_scalar(ang, ang, PI, -PI, ALU.min, ALU.max).then_inc(ang_ready, 1)
            dve.wait_ge(sin_ready, 2)
            half_s = work[:, 1, 0:SEQ]
            link(nc.vector.tensor_tensor(hi, half_s, half_s, ALU.mult))
            settle()
            link(nc.vector.tensor_scalar(cos_r[:, :, :], hi.rearrange("p (t n) -> p t n", t=TT), -2.0, 1.0,
                                         ALU.mult, ALU.add))
            settle()
            dve.wait_ge(small_in[2], 48)
            step4 = RD // HD
            for table, gi, scale in ((rope_q, 0, HD ** -0.5), (rope_k, 1, 1.0)):
                for kind, src in enumerate((cos_r, sin_r)):
                    for t in range(TT):
                        for hf in range(2):
                            o = table[:, kind, t, hf * 32:(hf + 1) * 32]
                            link(nc.vector.scalar_tensor_tensor(
                                out=o, in0=src[:, t, 0:P:step4], scalar=scale,
                                in1=gains[:, gi, hf * 32:(hf + 1) * 32], op0=ALU.mult, op1=ALU.mult))
            settle()

            def mean_square(k, src, cols, width):
                nc.vector.tensor_scalar(msq[:, 0:cols], src, 1.0 / width, EPS,
                                        ALU.mult, ALU.add).then_inc(ms_ready, 1)

            dve.wait_ge(ss_ready, 1)
            mean_square(1, xsum[:, :, 0], TT, D)
            dve.wait_ge(rstd_ready, 1)
            for t in range(TT):
                ins = nc.vector.tensor_scalar(res[:, t, :], res[:, t, :], rstd[:, t:t + 1], None, ALU.mult)
            ins.then_inc(norm_ready, 1)

            dve.wait_ge(vecs_ready, 1)
            dve.wait_ge(aux_freed[0], 1)
            dve.wait_ge(bias_landed, 32)
            def sums(i):
                for m in range(4):
                    for s in range(2):
                        for h in range(2):
                            k = 4 * m + 2 * s + h
                            dve.wait_ge(raw_landed[k % RAW], i * 32 + (16 * (k // RAW) + 16))
                            if k >= 4 or not isinstance(i, int):
                                dve.wait_ge(chunk_done, i * 16 + (k - 3))
                            dst = acc[:, s, h * CE:(h + 1) * CE]
                            nc.vector.scalar_tensor_tensor(
                                out=dst, in0=raw[:, k % RAW, :], scalar=vecs[:, 0, bass.ds(i * 4 + m, 1)],
                                in1=dst, op0=ALU.mult, op1=ALU.add).then_inc(chunk_done, 1)

            sums(0)
            with dve.Fori(1, KT // 4) as i:
                sums(i)

            def take_mod(k, filled, gain):
                dve.wait_ge(aux_filled[1], filled)
                link(nc.vector.tensor_copy(modB[:, :], aux_ps[:, 1, 0:KT]))
                link(nc.vector.scalar_tensor_tensor(out=modA[:, :], in0=aux_ps[:, 1, KT:2 * KT], scalar=1.0,
                                                    in1=vecs[:, gain, :], op0=ALU.add, op1=ALU.mult))
                settle()
                nc.vector.tensor_copy(den[:, 0, 0:1], modA[:, 0:1]).then_inc(aux_freed[1], 1)

            take_mod(0, 1, 1)

            def affine(k, filled):
                g, pair = k % 4, k % 2
                dve.wait_ge(aux_filled[pair], filled)
                if k >= 2:
                    dve.wait_ge(hT_ready, k - 1)
                for m in range(4):
                    kt = 4 * g + m
                    ins = nc.vector.tensor_scalar(tmp[:, pair, m * SEQ:(m + 1) * SEQ],
                                                  aux_ps[:, pair, m * SEQ:(m + 1) * SEQ],
                                                  modA[:, kt:kt + 1], modB[:, kt:kt + 1], ALU.mult, ALU.add)
                ins.then_inc(aux_freed[pair], 1)

            def low_h(k):
                dve.wait_ge(hT_high, k + 1)
                g = k % 4
                nc.vector.tensor_tensor(hT[:, 1, 4 * g:4 * g + 4, :],
                                        tmp[:, k % 2, :].rearrange("p (k n) -> p k n", k=4),
                                        hT[:, 0, 4 * g:4 * g + 4, :].bitcast(F32),
                                        ALU.subtract).then_inc(hT_ready, 1)

            def affine_all(k0, fills):
                affine(k0, fills[0])
                for g in range(1, 4):
                    affine(k0 + g, fills[g])
                    low_h(k0 + g - 1)
                low_h(k0 + 3)

            for k in range(AHEAD):
                low(R0, FIRST, k)
            affine_all(0, [2, 2, 3, 3])
            dve.wait_ge(bias_landed, 64)

            R_LINKS = 6
            with dve.Fori(0, R_TRIPS) as i:
                chain[0] = chain[0].over(i, R_LINKS)
                start = chain[0].fixed
                at = R0.over(i, R_N, R_W, R_B)
                bv, bq, bk, bg = r_blocks(i)
                a0, a1 = AUX_R

                def rope(slot, b):
                    dve.wait_ge(block_taken[b.slot(2)], taken(b))
                    xs = work[:, slot, :].rearrange("p (t h n) -> p t h n", t=TT, h=4)
                    for m, table in enumerate((cos_r, sin_r)):
                        link(nc.vector.tensor_tensor(
                            tmp[:, m, :].rearrange("p (t h n) -> p t h n", t=TT, h=4), xs,
                            table[:, :, :].unsqueeze(2).to_broadcast([P, TT, 4, P]), ALU.mult))
                    settle()
                    v = [y.rearrange("p (t h n) -> p t h n", h=2, n=P)
                         for y in (work[:, slot, :], tmp[:, 0, :], tmp[:, 1, :])]
                    link(nc.vector.tensor_tensor(v[0][:, :, 0, :], v[1][:, :, 0, :], v[2][:, :, 1, :], ALU.subtract))
                    settle()
                    nc.vector.tensor_tensor(v[0][:, :, 1, :], v[1][:, :, 1, :], v[2][:, :, 0, :],
                                            ALU.add).then_inc(roped, 1)

                step(at, bv)
                at = at.after(bv)
                step(at, bq)
                rope(0, at.b)
                at = at.after(bq)
                step(at, bk)
                rope(1, at.b)
                at = at.after(bk)

                def mask():
                    dve.wait_ge(aux_filled[0], i * 2 + (a0 + 2))
                    dve.wait_ge(decay_landed, i * 16 + 16)
                    dve.wait_ge(aux_filled[1], i * 2 + a1)
                    nc.vector.tensor_tensor(maskd[:, :, :],
                                            aux_ps[:, 0, :].rearrange("p (h n) -> p h n", h=2)[:, :, 0:3 * P],
                                            decay_sb[:, :, :], ALU.mult).then_inc(aux_freed[0], 1)

                step(at, bg, {9: mask})
                dve.wait_ge(ss_ready, i + 2)
                mean_square(0, ssum[:, 0:4], 4, RD)
                dve.wait_ge(rstd_ready, i + 2)
                dve.wait_ge(block_taken[at.b.slot(2)], taken(at.b))
                for t in range(TT):
                    for hd in range(2):
                        c0 = t * CB + hd * RD
                        ins = nc.vector.scalar_tensor_tensor(
                            out=res[:, t, bass.ds(i * CB + hd * RD, RD)], in0=aux_ps[:, 1, c0:c0 + RD],
                            scalar=rstd[:, 2 * t + hd:2 * t + hd + 1], in1=work[:, 3, c0:c0 + RD],
                            op0=ALU.mult, op1=ALU.mult)
                ins.then_inc(aux_freed[1], 1)
                assert chain[0].fixed == start + R_LINKS
            chain[0] = At(start + R_TRIPS * R_LINKS)

            def low_split(dst, k, pair, kt):
                dve.wait_ge(split_high, k)
                nc.vector.tensor_tensor(dst[:, 1, bass.ds(kt, 4), :],
                                        aux_ps[:, pair, :].rearrange("p (k n) -> p k n", k=4),
                                        dst[:, 0, bass.ds(kt, 4), :].bitcast(F32),
                                        ALU.subtract).then_inc(aux_freed[pair], 1)

            def own_take(at):
                dve.wait_ge(block_taken[at.b.slot(2)], taken(at.b))

            def merge(at, blk, j, k, slot=0):
                dve.wait_ge(w_used, (at.w + (blk.chunks + 1)).value())
                b = at.b + (-1 if k == 0 else -2)
                dve.wait_ge(block_taken[b.slot(2)], taken(b))
                q = at.b.slot(2)
                dst = res[:, :, bass.ds(j * CB, CB)]
                sg = (wslot(slot) if isinstance(slot, int) else
                      work[:, bass.ds(slot, 1), :].rearrange("p a (t n) -> p (a t) n", t=TT))
                if k == 0:
                    nc.vector.tensor_tensor(dst, gemm_ps[:, q, :, :], sg, ALU.mult).then_inc(block_taken[q], 1)
                    return
                t3 = tmp[:, 0, :].rearrange("p (t n) -> p t n", t=TT)
                nc.vector.tensor_tensor(t3, gemm_ps[:, q, :, :], sg, ALU.mult).then_inc(block_taken[q], 1)
                own_take(at)
                nc.vector.tensor_tensor(dst, dst, t3, ALU.add).then_inc(merged, 1)

            def gates(G, first_hooks, k, last_hooks=None):
                step(G.start, G.first, first_hooks)
                with dve.Fori(0, G_TRIPS) as j:
                    at = G.loop.over(j, G_N, G_W, G_B)
                    bo, bgt = G.trip(j)
                    step(at, bo)
                    merge(at, bo, j, k)
                    step(at.after(bo), bgt)
                step(G.last_at, G.last, last_hooks)
                merge(G.last_at, G.last, 3, k)

            gates(GA, {6: lambda: (take_mod(1, AUX_GA[1] + 1, 2), dve.wait_ge(bias_landed, 96),
                                   low_split(zT, 1, 0, 0)),
                       8: lambda: low_split(zT, 2, 1, 4),
                       9: lambda: low_split(zT, 3, 0, 8),
                       10: lambda: low_split(zT, 4, 1, 12)}, 0)

            def rms_begin(k):
                dve.wait_ge(q_squared, k + 1)
                link(nc.vector.tensor_reduce(ssum[:, 0:16], tmp[:, 1, :].rearrange("p (h n) -> p h n", n=HD),
                                             AXX, ALU.add))
                settle()
                mean_square(0, ssum[:, 0:16], 16, HD)

            def rms_rope(table):
                xs = work[:, 0, :].rearrange("p (t h n) -> p t h n", t=TT, h=8)
                for m in range(2):
                    link(nc.vector.tensor_tensor(
                        tmp[:, m, :].rearrange("p (t h n) -> p t h n", t=TT, h=8), xs,
                        table[:, m, :, :].unsqueeze(2).to_broadcast([P, TT, 8, HD]), ALU.mult))
                settle()
                v = [y.rearrange("p (t h n) -> p t h n", h=2, n=HD // 2)
                     for y in (work[:, 0, :], tmp[:, 0, :], tmp[:, 1, :])]
                link(nc.vector.tensor_tensor(v[0][:, :, 0, :], v[1][:, :, 0, :], v[2][:, :, 1, :], ALU.subtract))
                link(nc.vector.tensor_tensor(v[0][:, :, 1, :], v[1][:, :, 1, :], v[2][:, :, 0, :], ALU.add))
                settle()

            def rms_end(k):
                dve.wait_ge(rstd_ready, R_TRIPS + 2 + k)
                if k == 1:
                    dve.wait_ge(aux_filled[1], AUX_S[1] + 1)
                elif k:
                    dve.wait_ge(aux_filled[0], SW_FILL["q", k - 2])
                src = work[:, 0, :].rearrange("p (h n) -> p h n", n=HD)
                if k == 0:
                    dst = work[:, 1:3, :].rearrange("p a (h c n) -> p (a h) c n", c=2, n=HD)
                    for cpy in range(2):
                        ins = nc.vector.tensor_tensor(dst[:, :, cpy, :], src,
                                                      rstd[:, 0:16].unsqueeze(2).to_broadcast([P, 16, HD]), ALU.mult)
                else:
                    dst = work[:, 1, :].rearrange("p (h n) -> p h n", n=HD)
                    ins = nc.vector.tensor_tensor(dst, src, rstd[:, 0:16].unsqueeze(2).to_broadcast([P, 16, HD]),
                                                  ALU.mult)
                ins.then_inc(q_ready, 1)

            def maxima(g, t):
                dve.wait_ge(aux_filled[t], SW_FILL["l", g, t])
                L = aux_ps[:, t, :].rearrange("p (h j) -> p h j", h=8)
                if t == 0:
                    link(nc.vector.memset(L[0:CHUNK, :, CHUNK:P], NEG))
                    settle()
                link(nc.vector.tensor_reduce(smax[:, t, :], L, AXX, ALU.max))
                settle()
                sk = sink_b[:, 8 * g:8 * g + 8].rearrange("p (m e) -> p e m", e=2)
                top = smax[:, t, :].rearrange("p (e m) -> p e m", e=2)
                link(nc.vector.tensor_tensor(top, top, sk, ALU.max))
                settle()
                link(nc.vector.tensor_scalar(nmax[:, t, :], smax[:, t, :], -1.0, None, ALU.mult))
                nc.vector.tensor_tensor(dsink[:, t, :].rearrange("p (e m) -> p e m", e=2), sk, top, ALU.subtract).then_inc(max_ready, 1)

            def denominators(g, t):
                dve.wait_ge(exp_ready, 2 * g + t + 1)
                link(nc.vector.tensor_tensor(den[:, t, :], rowsum[:, t, :], esink[:, t, :], ALU.add))
                settle()
                nc.vector.reciprocal(rden[:, t, :], den[:, t, :]).then_inc(rden_ready, 1)

            def o_low(g, t):
                dve.wait_ge(o_high, 2 * g + t + 1)
                nc.vector.tensor_tensor(zT[:, 1, 4 * g:4 * g + 4, t * P:(t + 1) * P],
                                        aux_ps[:, t, 0:CB].rearrange("p (k n) -> p k n", k=4),
                                        zT[:, 0, 4 * g:4 * g + 4, t * P:(t + 1) * P].bitcast(F32),
                                        ALU.subtract).then_inc(aux_freed[t], 1)

            step(s_at[0], s_blocks[0])
            step(s_at[1], s_blocks[1])
            rms_begin(0)
            step(s_at[2], s_blocks[2], {4: lambda: rms_rope(rope_k), 5: lambda: rms_end(0)})
            rms_begin(1)
            for g in range(3):
                hooks = {4: lambda: rms_rope(rope_q), 5: lambda: rms_end(g + 1)}
                if g:
                    hooks[4] = lambda: (rms_rope(rope_q), denominators(g - 1, 1))
                    hooks[10] = lambda: (o_low(g - 1, 0), o_low(g - 1, 1))
                step(s_at[3 + g], s_blocks[3 + g], hooks)
                maxima(g, 0)
                maxima(g, 1)
                rms_begin(g + 2)
                denominators(g, 0)
            step(GB.first_at[0], GB.firsts[0],
                 {4: lambda: (rms_rope(rope_q), denominators(2, 1)), 5: lambda: rms_end(4),
                  10: lambda: (o_low(2, 0), o_low(2, 1))})
            maxima(3, 0)
            maxima(3, 1)
            denominators(3, 0)
            step(GB.first_at[1], GB.firsts[1],
                 {4: lambda: denominators(3, 1), 10: lambda: (o_low(3, 0), o_low(3, 1))})
            with dve.Fori(0, GB.TRIPS) as j:
                at = GB.loop.over(j, G_N, G_W, G_B)
                bo, bgt = GB.trip(j)
                step(at, bo)
                merge(at, bo, j, 4, j)
                step(at.after(bo), bgt)
            step(GB.last_at[0], GB.lasts[0])
            merge(GB.last_at[0], GB.lasts[0], 2, 4, 0)
            step(GB.last_at[1], GB.lasts[1], {7: lambda: low_split(hT, 5, 0, 0), 9: lambda: low_split(hT, 6, 1, 4),
                                              10: lambda: low_split(hT, 7, 0, 8)})
            merge(GB.last_at[1], GB.lasts[1], 3, 4, 1)

            def gate_rows(k):
                dve.wait_ge(aux_freed[0], AUX_O[0] + k)
                dve.wait_ge(aux_freed[1], AUX_O[1] + 1 + k)

            for j in range(4):
                step(o_at[j], o_blocks[j], {6: lambda: low_split(hT, 8, 1, 12)} if j == 0 else {})
                dve.wait_ge(w_used, (o_at[j].w + (NCH + 1)).value())
                if j == 0:
                    gate_rows(1)
                q = o_at[j].b.slot(2)
                t3 = tmp[:, 0, :].rearrange("p (t n) -> p t n", t=TT)
                nc.vector.tensor_tensor(
                    t3, gemm_ps[:, q, :, :],
                    acc[:, 0, j * CB:(j + 1) * CB].unsqueeze(1).to_broadcast([P, TT, CB]),
                    ALU.mult).then_inc(block_taken[q], 1)
                own_take(o_at[j])
                dve.wait_ge(x_again[j % 2], 16 * (j // 2 + 1))
                nc.vector.tensor_tensor(res[:, :, j * CB:(j + 1) * CB], t3,
                                        work[:, j % 2, :].rearrange("p (t n) -> p t n", t=TT),
                                        ALU.add).then_inc(x1_ready, 1)
            dve.wait_ge(ss_ready, 1 + R_TRIPS + 4)
            link(nc.vector.tensor_reduce(ssum[:, 0:TT], xsum[:, :, :], AXX, ALU.add))
            settle()
            mean_square(0, ssum[:, 0:TT], TT, D)
            dve.wait_ge(rstd_ready, R_TRIPS + 7)
            w4 = work[:, :, :].rearrange("p a n -> p (a n)").rearrange("p (t n) -> p t n", t=TT)
            for g in range(4):
                for t in range(TT):
                    c = slice(4 * g * P, 4 * (g + 1) * P)
                    ins = nc.vector.tensor_scalar(w4[:, t, c], res[:, t, c], rstd[:, t:t + 1], None, ALU.mult)
                ins.then_inc(norm_ready, 1)
                if g == 1:
                    affine(4, AUX_F[0] - 1)
            f0, f1 = AUX_F
            affine(5, f1 - 1)
            low_h(4)
            low_h(5)

            def glu(at, up, k):
                dve.wait_ge(w_used, (at.w + (up.chunks + 1)).value())
                dve.wait_ge(block_taken[(at.b + -1).slot(2)], taken(at.b + -1))
                q = at.b.slot(2)
                dve.wait_ge(aux_filled[1], k + (f1 - 1))
                nc.vector.tensor_tensor(work[:, 1, :].rearrange("p (t n) -> p t n", t=TT), gemm_ps[:, q, :, :],
                                        work[:, 0, :].rearrange("p (t n) -> p t n", t=TT),
                                        ALU.mult).then_inc(block_taken[q], 1)

            splits = 8
            for p, part in enumerate(parts):
                def ffn_pair(at, j, k, T=None):
                    gate, up = part.pair(j)
                    hooks = {9: T} if T else {}
                    if isinstance(k, int) and k == 0:
                        hooks = {4: lambda: (affine(6, f0), low_h(6)), 5: lambda: (affine(7, f1), low_h(7))}
                    step(at, gate, hooks)
                    at = at.after(gate)
                    step(at, up)
                    glu(at, up, k + 1)

                ffn_pair(part.start, 0, part.first)
                with dve.Fori(1, part.pairs) as j:
                    ffn_pair(shifted(part.loop, j), j, j + part.first,
                             lambda: low_split(zT, j + splits, 1, j * 4 - 4))
                splits += part.pairs
                for m, (at_, blk) in enumerate(zip(part.out_at, part.outs)):
                    last = p == len(parts) - 1
                    hooks = {6: lambda: low_split(zT, splits, 1, 4 * part.pairs - 4)} if m == 0 else {}
                    step(at_, blk, hooks, nxt=not (last and m == 3))
                    dve.wait_ge(w_used, (at_.w + (blk.chunks + 1)).value())
                    if p == 0 and m == 0:
                        gate_rows(2)
                    q = at_.b.slot(2)
                    t3 = tmp[:, 0, :].rearrange("p (t n) -> p t n", t=TT)
                    nc.vector.tensor_tensor(
                        t3, gemm_ps[:, q, :, :],
                        acc[:, 1, m * CB:(m + 1) * CB].unsqueeze(1).to_broadcast([P, TT, CB]),
                        ALU.mult).then_inc(block_taken[q], 1)
                    own_take(at_)
                    settle()
                    dst = res[:, :, m * CB:(m + 1) * CB]
                    ins = nc.vector.tensor_tensor(dst, dst, t3, ALU.add)
                    if last:
                        ins.then_inc(out_ready, 1)
                    else:
                        link(ins)

        @block.tensor
        def _(pe):
            def gemm(at, blk, src, hooks=None):
                hooks = hooks or {}
                q = at.b.slot(2)
                pe.wait_ge(block_taken[q], taken(at.b + -2))
                last_kt = blk.chunks * KC - 1
                for k in range(blk.chunks):
                    if k in hooks:
                        hooks[k]()
                    s = (at.w + k).slot(SPL)
                    pe.wait_ge(chunk_done, (at.n + (blk.offset(k) + 1)).value())
                    for m in range(KC):
                        kt = KC * k + m
                        for t in range(TT):
                            for a, b in ((0, 0), (0, 1), (1, 0)):
                                ins = nc.tensor.matmul(gemm_ps[:, q, t, :], src[:, a, kt, t * P:(t + 1) * P],
                                                       split[:, s, b, m, :], start=kt == 0 and a == 0 and b == 0,
                                                       stop=kt == last_kt and a == 1)
                    ins.then_inc(w_used, 1)
                if blk.chunks in hooks:
                    hooks[blk.chunks]()

            uses = [At(0), At(0)]

            def aux(pair):
                if uses[pair].loops or uses[pair].fixed:
                    pe.wait_ge(aux_freed[pair], uses[pair].value())
                uses[pair] = uses[pair] + 1

            def emptied(pair):
                pe.wait_ge(aux_freed[pair], uses[pair].value())

            def enter(reg, per_trip, first=0):
                before = [u.fixed for u in uses]
                for p in range(2):
                    uses[p] = At(before[p] - first * per_trip[p]).over(reg, per_trip[p])
                return before

            def leave(before, per_trip, trips):
                for p in range(2):
                    uses[p] = At(before[p] + per_trip[p] * trips)

            def transpose_group(pair, src):
                aux(pair)
                for m in range(4):
                    for t in range(TT):
                        ins = nc.tensor.transpose(aux_ps[:, pair, (m * TT + t) * P:(m * TT + t + 1) * P],
                                                  src[:, t, m * P:(m + 1) * P], ident[:, :])
                ins.then_inc(aux_filled[pair], 1)

            def mod_columns(pair):
                aux(pair)
                for s in range(2):
                    for kt in range(KT):
                        ins = nc.tensor.matmul(aux_ps[:, pair, s * KT + kt:s * KT + kt + 1],
                                               acc[:, s, kt * P:(kt + 1) * P], ones[:, 0:1],
                                               start=True, stop=True)
                ins.then_inc(aux_filled[pair], 1)

            def gate_rows(pair, a, h):
                aux(pair)
                for m in range(2):
                    c0 = h * CE + m * CB
                    ins = nc.tensor.matmul(aux_ps[:, pair, m * CB:(m + 1) * CB], ones[:, :], acc[:, a, c0:c0 + CB],
                                           start=True, stop=True)
                ins.then_inc(aux_filled[pair], 1)

            pe.wait_ge(consts_ready, 4)
            pe.wait_ge(small_in[0], 48)
            aux(0)
            nc.tensor.transpose(aux_ps[:, 0, 0:P], tmp[:, 0, 0:P], ident[:, :]).then_inc(aux_filled[0], 1)
            nc.tensor.transpose(aux_ps[:, 1, 0:P], ident[:, :], ident[:, :]).then_inc(w_used, 1)
            pe.wait_ge(w_used, 1)
            pe.wait_ge(chunk_done, N_ADA0)
            mod_columns(1)
            pe.wait_ge(norm_ready, 1)
            for g in range(4):
                transpose_group(g % 2, res[:, :, 4 * g * P:4 * (g + 1) * P])
            pe.wait_ge(hT_ready, 4)

            with pe.Fori(0, R_TRIPS) as i:
                before = enter(i, (2, 2))
                at = R0.over(i, R_N, R_W, R_B)
                bv, bq, bk, bg = r_blocks(i)

                def heads_to_T(slot, pair, k):
                    pe.wait_ge(roped, i * 2 + (k + 1))
                    aux(pair)
                    for f in range(4):
                        for t in range(TT):
                            ins = nc.tensor.transpose(aux_ps[:, pair, (f * TT + t) * P:(f * TT + t + 1) * P],
                                                      work[:, slot, t * CB + f * P:t * CB + (f + 1) * P], ident[:, :])
                    ins.then_inc(aux_filled[pair], 1)

                def scores():
                    emptied(1)
                    aux(0)
                    qT = heads[:, 0:2 * CB].rearrange("p (h f n) -> p h f n", h=2, f=2)
                    kT = heads[:, 2 * CB:4 * CB].rearrange("p (h f n) -> p h f n", h=2, f=2)
                    for hd in range(2):
                        for c0, k0, q0, width in ((0, 0, 0, SEQ), (SEQ, P, P, P)):
                            for f in range(2):
                                ins = nc.tensor.matmul(aux_ps[:, 0, hd * CB + c0:hd * CB + c0 + width],
                                                       kT[:, hd, f, k0:k0 + P], qT[:, hd, f, q0:q0 + width],
                                                       start=f == 0, stop=f == 1)
                    ins.then_inc(aux_filled[0], 1)

                def outputs():
                    emptied(0)
                    pe.wait_ge(block_taken[v_at.slot(2)], taken(v_at))
                    aux(1)
                    for t in range(TT):
                        for hd in range(2):
                            o = aux_ps[:, 1, t * CB + hd * RD:t * CB + (hd + 1) * RD]
                            for kt in range(t + 1):
                                s0 = t * P if kt == 0 else 2 * P
                                ins = nc.tensor.matmul(o, maskd[:, hd, s0:s0 + P],
                                                       work[:, 2, kt * CB + hd * RD:kt * CB + (hd + 1) * RD],
                                                       start=kt == 0, stop=kt == t)
                    ins.then_inc(aux_filled[1], 1)

                v_at = at.b
                gemm(at, bv, hT)
                at = at.after(bv)
                gemm(at, bq, hT)
                at = at.after(bq)
                gemm(at, bk, hT, {6: lambda: heads_to_T(0, 0, 0)})
                at = at.after(bk)
                gemm(at, bg, hT, {3: lambda: heads_to_T(1, 1, 1), 5: scores, 8: outputs})
            leave(before, (2, 2), R_TRIPS)

            def split_group(pair, src, kt):
                transpose_group(pair, src[:, :, kt * P:(kt + 4) * P])

            def gates_z(G, first_hooks, done, last_hooks=None):
                gemm(G.start, G.first, hT, first_hooks)
                done()
                with pe.Fori(0, G_TRIPS) as j:
                    at = G.loop.over(j, G_N, G_W, G_B)
                    bo, bgt = G.trip(j)
                    gemm(at, bo, zT)
                    gemm(at.after(bo), bgt, hT)
                gemm(G.last_at, G.last, zT, last_hooks)

            def first_y():
                emptied(1)

            gates_z(GA, {2: lambda: (first_y(), mod_columns(1), split_group(0, res, 0)),
                         3: lambda: split_group(1, res, 4),
                         5: lambda: split_group(0, res, 8), 6: lambda: split_group(1, res, 12)},
                    lambda: (emptied(0), emptied(1)))

            gemm(s_at[0], s_blocks[0], hT)
            gemm(s_at[1], s_blocks[1], hT)

            def keys_to_T():
                pe.wait_ge(q_ready, 1)
                kd = work[:, 1:3, :].rearrange("p t n -> p (t n)")
                for p in range(2):
                    aux(p)
                    for kv in range(4):
                        for t in range(TT):
                            c0 = t * 2 * CB + (4 * p + kv) * 2 * HD
                            ins = nc.tensor.transpose(aux_ps[:, p, (kv * TT + t) * P:(kv * TT + t + 1) * P],
                                                      kd[:, c0:c0 + P], ident[:, :])
                    ins.then_inc(aux_filled[p], 1)

            gemm(s_at[2], s_blocks[2], hT, {7: keys_to_T})
            kT = heads[:, :].rearrange("p (h n) -> p h n", n=SEQ)
            qT = work[:, 2, :].rearrange("p (h n) -> p h n", n=SEQ)

            def queries_to_T(g):
                pe.wait_ge(q_ready, g + 2)
                aux(0)
                for f in range(4):
                    for t in range(TT):
                        ins = nc.tensor.transpose(aux_ps[:, 0, (f * TT + t) * P:(f * TT + t + 1) * P],
                                                  work[:, 1, t * CB + f * P:t * CB + (f + 1) * P], ident[:, :])
                ins.then_inc(aux_filled[0], 1)

            def logits(g):
                emptied(0)
                emptied(1)
                for t in range(TT):
                    aux(t)
                    L = aux_ps[:, t, :].rearrange("p (h j) -> p h j", h=8)
                    for h in range(8):
                        s = h % 2 * HD
                        kv = 2 * g + h // 4
                        for par in range(2):
                            q0 = t * P + par * CHUNK
                            lhsT = qT[s:s + HD, h // 2, q0:q0 + CHUNK]
                            o = L[par * CHUNK:(par + 1) * CHUNK, h % 2 * 4 + h // 2, :]
                            if par == 1:
                                keys = ((0, t * P, P),)
                            elif t == 1:
                                keys = ((0, P, CHUNK), (CHUNK, CHUNK, CHUNK))
                            else:
                                keys = ((0, 0, CHUNK),)
                            for c0, k0, width in keys:
                                ins = nc.tensor.matmul(o[:, c0:c0 + width], lhsT, kT[s:s + HD, kv, k0:k0 + width],
                                                       start=True, stop=True)
                    ins.then_inc(aux_filled[t], 1)

            def probs_to_T(g, t):
                pe.wait_ge(probs_ready, 2 * g + t + 1)
                aux(t)
                for h in range(8):
                    ins = nc.tensor.transpose(aux_ps[:, t, h * P:(h + 1) * P], probs[:, t, h * P:(h + 1) * P],
                                              ident[:, :])
                ins.then_inc(aux_filled[t], 1)

            def attend(g, t):
                pe.wait_ge(vmix_ready, 2)
                aux(t)
                pT = probsT[:, t, :].rearrange("p (h n) -> p h n", h=8)
                o = aux_ps[:, t, 0:CB].rearrange("p (k n) -> p k n", k=4)
                for par in range(2):
                    for kvl in range(2):
                        v0 = (2 * g + kvl) * HD
                        if par == 1:
                            v = work[:, 3, t * CB + v0:t * CB + v0 + HD]
                        elif t == 1:
                            v = vmix[:, v0:v0 + HD]
                        else:
                            v = work[0:CHUNK, 3, v0:v0 + HD]
                        rows = CHUNK if (t, par) == (0, 0) else P
                        for e in range(2):
                            ins = nc.tensor.matmul(
                                o[e * HD:(e + 1) * HD, 2 * kvl:2 * kvl + 2, par * CHUNK:(par + 1) * CHUNK], v,
                                pT[0:rows, 4 * e + 2 * kvl:4 * e + 2 * kvl + 2, par * CHUNK:(par + 1) * CHUNK],
                                start=True, stop=True)
                ins.then_inc(aux_filled[t], 1)

            def attention(g):
                return {4: lambda: probs_to_T(g, 0), 5: lambda: probs_to_T(g, 1),
                        6: lambda: (attend(g, 0), attend(g, 1))}

            for g in range(3):
                hooks = attention(g - 1) if g else {}
                hooks.update({7: lambda: queries_to_T(g), 8: lambda: logits(g)})
                gemm(s_at[3 + g], s_blocks[3 + g], hT, hooks)
            gemm(GB.first_at[0], GB.firsts[0], hT,
                 {**attention(2), 7: lambda: queries_to_T(3), 8: lambda: logits(3)})
            gemm(GB.first_at[1], GB.firsts[1], hT, attention(3))
            emptied(0)
            emptied(1)
            with pe.Fori(0, GB.TRIPS) as j:
                at = GB.loop.over(j, G_N, G_W, G_B)
                bo, bgt = GB.trip(j)
                gemm(at, bo, zT)
                gemm(at.after(bo), bgt, hT)
            gemm(GB.last_at[0], GB.lasts[0], zT)
            gemm(GB.last_at[1], GB.lasts[1], zT,
                    {2: lambda: (pe.wait_ge(merged, 3), split_group(0, res, 0)),
                     4: lambda: split_group(1, res, 4),
                     6: lambda: split_group(0, res, 8)})

            def last_merged():
                pe.wait_ge(merged, 4)
                split_group(1, res, 12)

            emptied(0)
            emptied(1)
            gemm(o_at[0], o_blocks[0], hT, {2: last_merged,
                                            4: lambda: gate_rows(0, 0, 0),
                                            5: lambda: gate_rows(1, 0, 1)})
            gemm(o_at[1], o_blocks[1], hT, {4: lambda: gate_rows(0, 1, 0),
                                            5: lambda: gate_rows(1, 1, 1)})
            gemm(o_at[2], o_blocks[2], hT)
            gemm(o_at[3], o_blocks[3], hT)
            w4 = work[:, :, :].rearrange("p a n -> p (a n)").rearrange("p (t n) -> p t n", t=TT)

            def h2_group(g):
                pe.wait_ge(norm_ready, g + 2)
                split_group(g % 2, w4, 4 * g)

            h2_group(0)
            h2_group(1)
            h2_hooks = {0: lambda: pe.wait_ge(hT_ready, 5), 1: lambda: h2_group(2),
                        2: lambda: (h2_group(3), pe.wait_ge(hT_ready, 6)),
                        4: lambda: pe.wait_ge(hT_ready, 7), 6: lambda: pe.wait_ge(hT_ready, 8)}

            act3 = work[:, 1, :].rearrange("p (t n) -> p t n", t=TT)
            for p, part in enumerate(parts):
                gate, up = part.pair(0)
                gemm(part.start, gate, hT, h2_hooks if p == 0 else {})
                gemm(part.start.after(gate), up, hT)
                with pe.Fori(1, part.pairs) as j:
                    before = enter(j, (0, 1), 1)
                    at = shifted(part.loop, j)
                    gate, up = part.pair(j)

                    def group():
                        pe.wait_ge(block_taken[1], taken(at.b + -1))
                        transpose_group(1, act3)

                    gemm(at, gate, hT, {4: group})
                    gemm(at.after(gate), up, hT)
                leave(before, (0, 1), part.pairs - 1)

                def last_group():
                    pe.wait_ge(block_taken[1], taken(part.out_at[0].b + -1))
                    transpose_group(1, act3)

                for m, (at_, blk) in enumerate(zip(part.out_at, part.outs)):
                    tail = blk.chunks - 2
                    hooks = {0: lambda: emptied(1), 1: last_group, tail: lambda: emptied(1)} if m == 0 else {}
                    gemm(at_, blk, zT, hooks)


def _constants():
    inv_freq = (THETA ** (-np.arange(0, RD, 2) / RD)).astype(np.float32)[None, :]
    lg = np.log1p(-np.exp2(-5.0 - np.arange(RH)))
    i = np.arange(SEQ)
    seen = (i[:, None] // CHUNK) <= (i[None, :] // CHUNK)
    d = np.exp(lg[:, None, None] * np.abs(i[:, None] - i[None, :])) * seen * RD ** -0.5
    decay = np.concatenate([d[:, :P, :], d[:, P:, P:]], axis=2).transpose(1, 0, 2)
    return inv_freq, np.ascontiguousarray(decay.astype(np.float32))


_INS = ["x", "c", "positions", "w_ada", "b_ada", "norm_mix_gain", "w_in", "q_norm_gain", "k_norm_gain",
        "sinks", "w_ret_out", "w_swa_out", "w_o", "norm_ffn_gain", "w_ffn_in", "w_ffn_out"]


def kernel(**inputs):
    import concourse.bacc as bacc
    from concourse.bass_utils import run_bass_kernel_spmd

    nc = bacc.Bacc("TRN2", target_bir_lowering=False, num_devices=1, dynamic_dma_scratch_size=2048)
    inv_freq, decay = _constants()
    arrays, args = {}, []
    given = [(name, np.ascontiguousarray(inputs[name])) for name in _INS]
    for name, a in given + [("inv_freq", inv_freq), ("decay", decay)]:
        arrays[f"in_{name}"] = a
        args.append(nc.dram_tensor(f"in_{name}", a.shape, mybir.dt.from_np(a.dtype), kind="ExternalInput").ap())
    out = nc.dram_tensor("out", (1, SEQ, D), F32, kind="ExternalOutput").ap()
    hybrid_block_kernel(nc, *args, out)
    r = run_bass_kernel_spmd(nc, [arrays], core_ids=[0])
    return r.results[0]["out"]
```

```python
from contextlib import ExitStack

import numpy as np

import concourse.bass as bass
from concourse import mybir

F32 = mybir.dt.float32
F32R = mybir.dt.float32r
I32 = mybir.dt.int32
ALU = mybir.AluOpType
ACT = mybir.ActivationFunctionType
AXX = mybir.AxisListType.X

P = 128
D = 2048
SEQ = 256
TT = SEQ // P
KT = D // P
CB = 512
CHUNK = 64
RH, RD = 8, 256
QH, KVH, HD = 32, 8, 64
D_FF = 5632
EPS = 1e-6
THETA = 10000.0
NEG = -1e30
KC = 2
CE = KC * CB
RAW = 8
SPL = 4
AHEAD = 3
NCH = KT // KC

C_RQ, C_RK, C_RV, C_RG = 0, D, 2 * D, 3 * D
C_AQ, C_AK, C_AV = 4 * D, 5 * D, 5 * D + KVH * HD
C_GA, C_GB = 5 * D + 2 * KVH * HD, 6 * D + 2 * KVH * HD
SHIFT1, SCALE1, GATE1, SHIFT2, SCALE2, GATE2 = range(6)

_TP = 2.0 * np.pi
TP1 = float(np.floor(_TP * 2 ** 9) / 2 ** 9)
TP2 = float(np.floor((_TP - TP1) * 2 ** 21) / 2 ** 21)
TP3 = float(np.float32(_TP - TP1 - TP2))
ROUND = float(1.5 * 2 ** 23)
ROUND_HI = ROUND * 2048.0


class At:

    def __init__(self, fixed, loops=()):
        self.fixed, self.loops = fixed, tuple(loops)

    def __add__(self, k):
        return At(self.fixed + k, self.loops)

    def over(self, reg, stride):
        if isinstance(reg, int):
            return self + reg * stride
        return At(self.fixed, self.loops + ((reg, stride),)) if stride else self

    def value(self, times=1, per=1):
        v = (self.fixed // per) * times
        for reg, stride in self.loops:
            assert stride % per == 0
            v = reg * (stride // per * times) + v
        return v

    def slot(self, size):
        assert all(stride % size == 0 for _, stride in self.loops)
        return self.fixed % size


class Place:

    def __init__(self, n=0, w=0, b=0):
        self.n, self.w, self.b = [x if isinstance(x, At) else At(x) for x in (n, w, b)]

    def over(self, reg, n, w, b):
        return Place(self.n.over(reg, n), self.w.over(reg, w), self.b.over(reg, b))

    def after(self, block):
        return Place(self.n + block.raws, self.w + block.chunks, self.b + 1)


class Block:

    def __init__(self, weights, col, rows=0, chunks=NCH, ada=((), ())):
        self.weights, self.col, self.rows, self.chunks, self.ada = weights, col, rows, chunks, ada
        self.raws = chunks + len(ada[0]) + len(ada[1])

    def offset(self, k):
        return k + (len(self.ada[0]) if k >= 4 else 0)

    def ada_after(self, k):
        return self.ada[0] if k == 3 else self.ada[1] if k == 7 else ()


N_ADA0 = KT * 4
QUARTERS = 4
Q_LEAD = 5
Q_MOD = 2
R_TRIPS, R_N, R_W, R_B = 4, 48, 32, 4
G_TRIPS, G_N, G_W, G_B = 3, 24, 16, 2
F_N, F_W, F_B = 16, 16, 2


def r_blocks(i):
    out = []
    for m, c in enumerate((C_RV, C_RQ, C_RK, C_RG)):
        ada = tuple([(s, SHIFT2 + s, i * 4 + m, h) for h in range(2)] for s in range(2))
        out.append(Block("w_in", (i + c // CB) * CB, ada=ada))
    return out


def prologue_stream():
    ada = [[("ada", g, kt) for kt in range(KT)] for g in range(QUARTERS)]
    weights = [[("w", g, k) for k in range(4)] for g in range(QUARTERS)]
    out = list(ada[0])
    for g in range(1, QUARTERS):
        out += ada[g][:Q_LEAD] + weights[g - 1] + ada[g][Q_LEAD:]
    return out + weights[-1]


def first_tail():
    return [Block("w_in", c, ada=tuple([(s, SHIFT2 + s, 2 * m + g, h) for s in range(2) for h in range(2)]
                                       for g in range(2)))
            for m, c in enumerate((C_RK, C_RG))]


def gate_ada(acc, section, m):
    if isinstance(m, int) and m == 0:
        return (), tuple([(acc, section, g, h) for g in range(2) for h in range(2)])
    return tuple([(acc, section, m * 2 + g, h) for h in range(2)] for g in range(2))


def ffn_parts():
    n = D_FF // CB
    return [(4 * p, min(4, n - 4 * p)) for p in range(-(-n // 4))]


def sliding_window_fills(first0, first1):
    n, out = [first0, first1], {}

    def use(key, pair):
        n[pair] += 1
        out[key] = n[pair]

    def rest(g):
        for kind in "po":
            for t in range(2):
                use((kind, g, t), t)

    for g in range(4):
        if g:
            rest(g - 1)
        use(("q", g), 0)
        use(("l", g, 0), 0)
        use(("l", g, 1), 1)
    rest(3)
    return out, tuple(n)


def hybrid_block_kernel(nc, x, c, positions, w_ada, b_ada, norm_mix_gain, w_in, q_norm_gain,
                        k_norm_gain, sinks, w_ret_out, w_swa_out, w_o, norm_ffn_gain, w_ffn_in,
                        w_ffn_out, inv_freq, decay, out):
    x_v = x.rearrange("o (t p) n -> p (o t) n", p=P)
    out_v = out.rearrange("o (t p) n -> p (o t) n", p=P)
    rows_v = {
        name: w.rearrange("o (k p) n -> p (o k) n", p=P)
        for name, w in (("w_ada", w_ada), ("w_in", w_in), ("w_ret_out", w_ret_out),
                        ("w_swa_out", w_swa_out), ("w_o", w_o), ("w_ffn_in", w_ffn_in),
                        ("w_ffn_out", w_ffn_out))
    }

    with ExitStack() as ctx:
        def sb(name, shape, dt=F32):
            return ctx.enter_context(nc.sbuf_tensor(name, shape, dt))

        def sem(name):
            return ctx.enter_context(nc.semaphore(name))

        raw = sb("raw", [P, RAW, CE])
        split = sb("split", [P, SPL, 2, KC, CB], F32R)
        res = sb("res", [P, TT, D])
        hT = sb("hT", [P, 2, KT, SEQ], F32R)
        zT = sb("zT", [P, 2, KT, SEQ], F32R)
        acc = sb("acc", [P, 2, D])
        work = sb("work", [P, 4, 2 * CB])
        tmp = sb("tmp", [P, 2, 2 * CB])
        heads = sb("heads", [P, 2 * 2 * CB])
        maskd = sb("maskd", [P, 2, 3 * P])
        decay_sb = sb("decay_sb", [P, 2, 3 * P])
        probs = sb("probs", [P, 2, 2 * CB])
        probsT = sb("probsT", [P, 2, 2 * CB])
        vmix = maskd[:, :, :].rearrange("p h n -> p (h n)")[:, 0:CB]
        cos_r = sb("cos_r", [P, TT, P])
        sin_r = sb("sin_r", [P, TT, P])
        rope_q = sb("rope_q", [P, 2, TT, HD])
        rope_k = sb("rope_k", [P, 2, TT, HD])
        gains = sb("gains", [P, 2, HD])
        ident = sb("ident", [P, P])
        ones = sb("ones", [P, P])
        vecs = sb("vecs", [P, 3, KT])
        modA = sb("modA", [P, KT])
        modB = sb("modB", [P, KT])
        pos_i = sb("pos_i", [P, TT], I32)
        pos_f = sb("pos_f", [P, TT])
        sink_b = sb("sink_b", [P, QH])
        minus_half = sb("minus_half", [P, 16])
        ssum = sb("ssum", [P, 16])
        msq = sb("msq", [P, 16])
        rstd = sb("rstd", [P, 16])
        xsum = sb("xsum", [P, TT, 4])
        smax = sb("smax", [P, 2, 8])
        nmax = sb("nmax", [P, 2, 8])
        dsink = sb("dsink", [P, 2, 8])
        esink = sb("esink", [P, 2, 8])
        rowsum = sb("rowsum", [P, 2, 8])
        den = sb("den", [P, 2, 8])
        rden = sb("rden", [P, 2, 8])

        gemm_ps = ctx.enter_context(nc.psum_tensor("gemm_ps", [P, 2, TT, CB], F32))
        aux_ps = ctx.enter_context(nc.psum_tensor("aux_ps", [P, 2, 2 * CB], F32))

        small_in = [sem(f"small_in{k}") for k in range(3)]
        raw_landed = [sem(f"raw_landed{k}") for k in range(RAW)]
        x_landed = sem("x_landed")
        x_again = [sem(f"x_again{k}") for k in range(2)]
        decay_landed = sem("decay_landed")
        bias_landed = sem("bias_landed")
        stored = sem("stored")
        consts_ready = sem("consts_ready")
        acc_zeroed = sem("acc_zeroed")
        high_ready = sem("high_ready")
        chunk_done = sem("chunk_done")
        w_used = sem("w_used")
        block_taken = [sem(f"block_taken{k}") for k in range(2)]
        aux_filled = [sem(f"aux_filled{k}") for k in range(2)]
        aux_freed = [sem(f"aux_freed{k}") for k in range(2)]
        dve_chain = sem("dve_chain")
        vecs_ready = sem("vecs_ready")
        ss_ready = sem("ss_ready")
        ms_ready = sem("ms_ready")
        rstd_ready = sem("rstd_ready")
        norm_ready = sem("norm_ready")
        own_affine = sem("own_affine")
        hT_high = sem("hT_high")
        hT_ready = sem("hT_ready")
        split_high = sem("split_high")
        ang_ready = sem("ang_ready")
        sin_ready = sem("sin_ready")
        roped = sem("roped")
        merged = sem("merged")
        vmix_ready = sem("vmix_ready")
        q_squared = sem("q_squared")
        q_ready = sem("q_ready")
        max_ready = sem("max_ready")
        exp_ready = sem("exp_ready")
        rden_ready = sem("rden_ready")
        probs_ready = sem("probs_ready")
        o_high = sem("o_high")
        x1_ready = sem("x1_ready")
        out_ready = sem("out_ready")

        STREAM = prologue_stream()
        R0 = Place(N_ADA0)
        TAIL0 = Place(len(STREAM), QUARTERS * 4, 2)
        V0, Q0 = Place(w=QUARTERS * 4 - 10), Place(w=QUARTERS * 4 - 8, b=1)
        G0 = Place(N_ADA0 + R_TRIPS * R_N, R_TRIPS * R_W, R_TRIPS * R_B)

        class Gate:

            def __init__(self, start, col, w_out, a, section):
                self.start, self.col, self.w_out, self.a, self.section = start, col, w_out, a, section
                self.first = Block("w_in", col, ada=gate_ada(a, section, 0))
                self.loop = start.after(self.first)
                self.last = Block(w_out, 3 * CB, ada=gate_ada(a, section, 7))
                n = self.loop
                self.last_at = Place(n.n + G_TRIPS * G_N, n.w + G_TRIPS * G_W, n.b + G_TRIPS * G_B)
                self.end = self.last_at.after(self.last)

            def trip(self, j):
                return [Block(self.w_out, j * CB, ada=gate_ada(self.a, self.section, j * 2 + 1)),
                        Block("w_in", j * CB + (self.col + CB), ada=gate_ada(self.a, self.section, j * 2 + 2))]

        GA = Gate(G0, C_GA, "w_ret_out", 0, GATE1)
        s_blocks = [Block("w_in", C_AV), Block("w_in", C_AK)] + [
            Block("w_in", C_AQ + g * CB) for g in range(4)]
        s_at = [GA.end]
        for blk in s_blocks:
            s_at.append(s_at[-1].after(blk))

        class LateGate:

            TRIPS = 2

            def __init__(self, start, col, w_out, a, section):
                self.col, self.w_out, self.a, self.section = col, w_out, a, section
                self.firsts = [Block("w_in", col + m * CB, ada=self.ada(m)) for m in range(2)]
                self.lasts = [Block(w_out, m * CB, ada=self.ada(4 + m)) for m in (2, 3)]
                self.first_at = [start, start.after(self.firsts[0])]
                self.loop = n = self.first_at[1].after(self.firsts[1])
                t = self.TRIPS
                self.last_at = [Place(n.n + t * G_N, n.w + t * G_W, n.b + t * G_B)]
                self.last_at.append(self.last_at[0].after(self.lasts[0]))
                self.end = self.last_at[1].after(self.lasts[1])

            def ada(self, m):
                return tuple([(self.a, self.section, m * 2 + g, h) for h in range(2)] for g in range(2))

            def trip(self, j):
                return [Block(self.w_out, j * CB, ada=self.ada(j * 2 + 2)),
                        Block("w_in", j * CB + (self.col + 2 * CB), ada=self.ada(j * 2 + 3))]

        GB = LateGate(s_at[-1], C_GB, "w_swa_out", 1, GATE2)
        o_blocks = [Block("w_o", j * CB) for j in range(4)]
        o_at = [GB.end]
        for blk in o_blocks:
            o_at.append(o_at[-1].after(blk))

        class Part:

            def __init__(self, start, first, pairs):
                self.start, self.first, self.pairs = start, first, pairs
                self.loop = start.after(Block("w_ffn_in", 0)).after(Block("w_ffn_in", 0))
                k = pairs - 1
                self.out_at = [Place(self.loop.n + k * F_N, self.loop.w + k * F_W, self.loop.b + k * F_B)]
                self.outs = [Block("w_ffn_out", j * CB, rows=first * 4, chunks=pairs * 4 // KC) for j in range(4)]
                for blk in self.outs:
                    self.out_at.append(self.out_at[-1].after(blk))

            def pair(self, j):
                col = (self.first + j) * CB if isinstance(j, int) else j * CB + self.first * CB
                return [Block("w_ffn_in", col), Block("w_ffn_in", col + D_FF)]

        parts, at = [], o_at[-1]
        for first, pairs in ffn_parts():
            parts.append(Part(at, first, pairs))
            at = parts[-1].out_at[-1]

        def shifted(loop, j):
            return Place(*[At(v.fixed - s, v.loops).over(j, s)
                           for v, s in ((loop.n, F_N), (loop.w, F_W), (loop.b, F_B))])

        def taken(b):
            return (b + 4).value(1, 2)

        AUX_R = (5, 4)
        AUX_GA = (AUX_R[0] + 8, AUX_R[1] + 8)
        AUX_S = (AUX_GA[0] + 3, AUX_GA[1] + 2)
        SW_FILL, AUX_GB = sliding_window_fills(AUX_S[0] + 1, AUX_S[1] + 1)
        AUX_O = (AUX_GB[0] + 2, AUX_GB[1] + 1)
        AUX_F = (AUX_O[0] + 4, AUX_O[1] + 5)

        def wslot(k):
            return work[:, k, :].rearrange("p (t n) -> p t n", t=TT)

        inv_freq_sb, angles = probs[:, 0, 0:P], probs[:, 0, SEQ:2 * SEQ]
        half_sin, turns_hi, turns_lo = [probs[:, 1, k * SEQ:(k + 1) * SEQ] for k in range(3)]

        block = ctx.enter_context(nc.Block())

        @block.sync
        def _(sp):
            sp.wait_ge(consts_ready, 3)
            for k, v in enumerate((c, norm_mix_gain, norm_ffn_gain)):
                sp.dma_start(tmp[16 * k:16 * k + 16, 0, 0:P],
                             v.rearrange("o (k p) -> (o k) p", p=P)).then_inc(small_in[0], 16)
            with nc.allow_non_contiguous_dma(reason="256 positions"):
                sp.dma_start(pos_i[:, :], positions.rearrange("o (t p) -> p (o t)", p=P)).then_inc(small_in[1], 16)
            sp.dma_start(inv_freq_sb, inv_freq.to_broadcast([P, P])).then_inc(small_in[1], 16)
            sp.dma_start(gains[:, 0, :], q_norm_gain.to_broadcast([P, HD])).then_inc(small_in[2], 16)
            sp.dma_start(gains[:, 1, :], k_norm_gain.to_broadcast([P, HD])).then_inc(small_in[2], 16)
            sp.dma_start(sink_b[:, :], sinks.to_broadcast([P, QH])).then_inc(small_in[2], 16)

            def load(n, src):
                if n.loops or n.fixed >= RAW:
                    sp.wait_ge(chunk_done, (n + (1 - RAW)).value())
                s = n.slot(RAW)
                dst = raw[:, s, :].rearrange("p (k n) -> p k n", k=src.shape[1])
                sp.dma_start(dst, src).then_inc(raw_landed[s], 16)

            def load_ada(n, section, kt, half):
                load(n, rows_v["w_ada"][:, bass.ds(kt, 1), section * D + half * CE:section * D + (half + 1) * CE])

            def load_block(at, blk):
                r = 0
                for k in range(blk.chunks):
                    kt = blk.rows + KC * k
                    load(at.n + r, rows_v[blk.weights][:, kt:kt + KC, bass.ds(blk.col, CB)])
                    r += 1
                    for _, section, akt, half in blk.ada_after(k):
                        load_ada(at.n + r, section, akt, half)
                        r += 1

            def load_all(at, blks):
                for blk in blks:
                    load_block(at, blk)
                    at = at.after(blk)

            for n, (kind, g, k) in enumerate(STREAM):
                if n == RAW:
                    sp.dma_start(res[:, :, :], x_v).then_inc(x_landed, 16)
                if kind == "ada":
                    load(At(n), w_ada.rearrange("o (k p) (s n) -> p (o k) s n", p=P, n=D)[
                        :, k, SHIFT1:SCALE1 + 1, g * CB:(g + 1) * CB])
                else:
                    col, kt = (C_RV, C_RQ)[k // 2], 4 * g + KC * (k % 2)
                    load(At(n), rows_v["w_in"][:, kt:kt + KC, col:col + CB])
            bk, bg = first_tail()
            load_block(TAIL0, bk)
            sp.dma_start(decay_sb[:, :, :], decay[:, 0:2, :]).then_inc(decay_landed, 16)
            load_block(TAIL0.after(bk), bg)
            with sp.Fori(1, R_TRIPS) as i:
                at, blks = R0.over(i, R_N, R_W, R_B), r_blocks(i)
                load_block(at, blks[0])
                head = i * 2
                sp.wait_ge(aux_freed[0], i * 2 + AUX_R[0])
                sp.dma_start(decay_sb[:, :, :], decay[:, bass.ds(head, 2), :]).then_inc(decay_landed, 16)
                load_all(at.after(blks[0]), blks[1:])

            def load_gate(G):
                load_block(G.start, G.first)
                with sp.Fori(0, G_TRIPS) as j:
                    load_all(G.loop.over(j, G_N, G_W, G_B), G.trip(j))
                load_block(G.last_at, G.last)

            load_gate(GA)
            for at_, blk in zip(s_at, s_blocks):
                load_block(at_, blk)
            load_all(GB.first_at[0], GB.firsts)
            with sp.Fori(0, GB.TRIPS) as j:
                load_all(GB.loop.over(j, G_N, G_W, G_B), GB.trip(j))
            load_all(GB.last_at[0], GB.lasts)
            for j, (at_, blk) in enumerate(zip(o_at, o_blocks)):
                load_block(at_, blk)
                if j == 0:
                    sp.wait_ge(merged, 4)
                if j >= 2:
                    sp.wait_ge(x1_ready, j - 1)
                sp.dma_start(work[:, j % 2, :].rearrange("p (t n) -> p t n", t=TT),
                             x_v[:, :, j * CB:(j + 1) * CB]).then_inc(x_again[j % 2], 16)
            for part in parts:
                load_all(part.start, part.pair(0))
                with sp.Fori(1, part.pairs) as j:
                    load_all(shifted(part.loop, j), part.pair(j))
                for at_, blk in zip(part.out_at, part.outs):
                    load_block(at_, blk)
            pieces = [(j, 0, TT) for j in range(3)] + [(3, 0, 1), (3, 1, TT)]
            for k, (j, t0, t1) in enumerate(pieces):
                sp.wait_ge(out_ready, k + 1)
                sp.dma_start(out_v[:, t0:t1, j * CB:(j + 1) * CB],
                             res[:, t0:t1, j * CB:(j + 1) * CB]).then_inc(stored, 16)
            sp.wait_ge(stored, 16 * len(pieces))

        @block.gpsimd
        def _(pool):
            nc.gpsimd.memset(ident[:, :], 0.0).then_inc(consts_ready, 1)
            nc.gpsimd.memset(ones[:, :], 1.0).then_inc(consts_ready, 1)
            nc.gpsimd.memset(tmp[:, 0, 0:P], 0.0).then_inc(consts_ready, 1)
            pool.wait_ge(consts_ready, 1)
            nc.gpsimd.affine_select(out=ident[:, :], in_=ident[:, :], compare_op=ALU.not_equal, fill=1.0,
                                    base=0, pattern=[[-1, P]], channel_multiplier=1).then_inc(consts_ready, 1)
            nc.gpsimd.memset(minus_half[:, :], -0.5).then_inc(consts_ready, 1)
            zeroed = [0]

            def start_acc(a, section):
                nc.gpsimd.memset(acc[:, a, :], 0.0).then_inc(acc_zeroed, 1)
                zeroed[0] += 1
                pool.wait_ge(acc_zeroed, zeroed[0])
                pool.dma_start(acc[0:1, a, :], b_ada[:, section * D:(section + 1) * D]).then_inc(bias_landed, 16)

            def rsqrt(k, cols):
                pool.wait_ge(ms_ready, k)
                nc.gpsimd.tensor_tensor(rstd[:, 0:cols], msq[:, 0:cols], minus_half[:, 0:cols],
                                        ALU.pow).then_inc(rstd_ready, 1)

            start_acc(0, SHIFT1)
            start_acc(1, SCALE1)
            pool.wait_ge(consts_ready, 5)
            rsqrt(1, TT)
            pool.wait_ge(aux_filled[1], AUX_R[1])
            start_acc(0, SHIFT2)
            start_acc(1, SCALE2)
            with pool.Fori(0, R_TRIPS) as i:
                rsqrt(i + 2, 4)
            pool.wait_ge(aux_filled[0], AUX_GA[0] + 1)
            start_acc(0, GATE1)
            start_acc(1, GATE2)
            pool.wait_ge(block_taken[s_at[0].b.slot(2)], taken(s_at[0].b))
            v = work[:, 3, :].rearrange("p (t n) -> p t n", t=TT)
            nc.gpsimd.tensor_copy(vmix[0:CHUNK, :], v[0:CHUNK, 1, :]).then_inc(vmix_ready, 1)
            pool.wait_ge(vmix_ready, 1)
            nc.gpsimd.tensor_copy(vmix[CHUNK:P, :], v[CHUNK:P, 0, :]).then_inc(vmix_ready, 1)
            pool.wait_ge(vmix_ready, 2)

            def square(k):
                b = s_at[1 + k].b
                pool.wait_ge(block_taken[b.slot(2)], taken(b))
                nc.gpsimd.tensor_tensor(tmp[:, 1, :], work[:, 0, :], work[:, 0, :], ALU.mult).then_inc(q_squared, 1)

            def normalise(k):
                pool.wait_ge(rden_ready, k + 1)
                p3 = probs[:, k % 2, :].rearrange("p (h j) -> p h j", h=8)
                nc.gpsimd.tensor_tensor(p3, p3, rden[:, k % 2, :].unsqueeze(2).to_broadcast([P, 8, P]),
                                        ALU.mult).then_inc(probs_ready, 1)

            square(0)
            rsqrt(R_TRIPS + 2, 16)
            square(1)
            rsqrt(R_TRIPS + 3, 16)
            for g in range(4):
                if g < 3:
                    square(g + 2)
                normalise(2 * g)
                if g < 3:
                    rsqrt(R_TRIPS + 4 + g, 16)
                normalise(2 * g + 1)
            rsqrt(R_TRIPS + 7, TT)

        @block.scalar
        def _(act):
            def prep(at, blk, k):
                n, w = at.n + blk.offset(k), at.w + k
                s, r = w.slot(SPL), n.slot(RAW)
                act.wait_ge(raw_landed[r], (n + RAW).value(16, RAW))
                if w.loops or w.fixed >= SPL:
                    act.wait_ge(w_used, (w + (2 - SPL)).value())
                nc.scalar.activation(split[:, s, 0, :, :], raw[:, r, :].rearrange("p (k n) -> p k n", k=KC),
                                     ACT.Copy).then_inc(high_ready, 1)

            def step(at, blk, hooks=None, nxt=True):
                hooks = hooks or {}
                for k in range(AHEAD, blk.chunks + (AHEAD if nxt else 0)):
                    if k in hooks:
                        hooks[k]()
                    if k < blk.chunks:
                        prep(at, blk, k)
                    else:
                        prep(at.after(blk), FIRST, k - blk.chunks)

            def take(at, blk, out, func):
                act.wait_ge(w_used, (at.w + (blk.chunks + 1)).value())
                q = at.b.slot(2)
                return nc.scalar.activation(out, gemm_ps[:, q, :, :], func).then_inc(block_taken[q], 1)

            act.wait_ge(aux_filled[0], 1)
            nc.scalar.activation(vecs[:, 0, :], aux_ps[:, 0, 0:KT], ACT.Silu).then_inc(vecs_ready, 1)
            act.wait_ge(vecs_ready, 1)
            nc.scalar.activation(vecs[:, 1:3, :], aux_ps[:, 0, KT:3 * KT].rearrange("p (a b) -> p a b", a=2),
                                 ACT.Copy).then_inc(aux_freed[0], 1)
            act.wait_ge(ang_ready, 1)
            nc.scalar.activation(sin_r[:, :, :], angles.rearrange("p (t n) -> p t n", t=TT),
                                 ACT.Sin).then_inc(sin_ready, 1)
            nc.scalar.activation(half_sin, angles, ACT.Sin, scale=0.5).then_inc(sin_ready, 1)
            act.wait_ge(x_landed, 16)
            for t in range(TT):
                nc.scalar.activation(gemm_ps[:, :, :, :].rearrange("p a b n -> p (a b n)"), res[:, t, :],
                                     ACT.Square, accum_out=ssum[:, t:t + 1]).then_inc(block_taken[t], 1)
                act.wait_ge(block_taken[t], 1)
            nc.scalar.activation(xsum[:, :, 0], ssum[:, 0:TT], ACT.Copy).then_inc(ss_ready, 1)
            act.wait_ge(rstd_ready, 1)
            for t in range(TT):
                ins = nc.scalar.activation(res[:, t, :], res[:, t, :], ACT.Copy, scale=rstd[:, t:t + 1])
            ins.then_inc(norm_ready, 1)

            def high_h(k, pair, filled):
                act.wait_ge(aux_freed[pair], filled)
                g = k % 4
                nc.scalar.activation(hT[:, 0, 4 * g:4 * g + 4, :],
                                     tmp[:, k % 2, :].rearrange("p (k n) -> p k n", k=4),
                                     ACT.Copy).then_inc(hT_high, 1)

            FIRST = Block("", 0)
            for g in range(QUARTERS):
                act.wait_ge(aux_filled[0], g + 2)
                act.wait_ge(aux_freed[1], g + 1)
                if g >= 2:
                    act.wait_ge(hT_ready, g - 1)
                for m in range(4):
                    kt = 4 * g + m
                    ins = nc.scalar.activation(tmp[:, g % 2, m * SEQ:(m + 1) * SEQ],
                                               aux_ps[:, 0, m * SEQ:(m + 1) * SEQ], ACT.Identity,
                                               bias=modB[:, kt:kt + 1], scale=modA[:, kt:kt + 1])
                ins.then_inc(aux_freed[0], 1)
                high_h(g, 0, g + 2)
                for k in range(4):
                    prep(Place(STREAM.index(("w", g, 0)), 4 * g), FIRST, k)
            for k in range(AHEAD):
                prep(TAIL0, FIRST, k)
            take(V0, FIRST, wslot(2), ACT.Copy)
            take(Q0, FIRST, wslot(0), ACT.Copy)

            def high_split(dst, pair, filled, kt):
                act.wait_ge(aux_filled[pair], filled)
                nc.scalar.activation(dst[:, 0, bass.ds(kt, 4), :],
                                     aux_ps[:, pair, :].rearrange("p (k n) -> p k n", k=4),
                                     ACT.Copy).then_inc(split_high, 1)

            a0, a1 = AUX_R

            def filled(i, pair, k):
                return i * 2 + ((a0, a1)[pair] + k + 1)

            def take_heads(i, pair):
                act.wait_ge(aux_filled[pair], filled(i, pair, 0))
                nc.scalar.activation(heads[:, pair * 2 * CB:(pair + 1) * 2 * CB], aux_ps[:, pair, :],
                                     ACT.Copy).then_inc(aux_freed[pair], 1)

            def retention_tail(i, at, bk, bg):
                step(at, bk, {10: lambda: take_heads(i, 0)})
                act.wait_ge(aux_filled[1], filled(i, 1, -2))
                take(at, bk, wslot(1), ACT.Copy)
                at = at.after(bk)
                step(at, bg, {7: lambda: take_heads(i, 1)})
                act.wait_ge(aux_freed[1], i * 2 + a1)
                take(at, bg, wslot(3), ACT.Silu)
                act.wait_ge(aux_filled[1], filled(i, 1, 1))
                for t in range(TT):
                    for hd in range(2):
                        ins = nc.scalar.activation(probs[:, hd, t * RD:(t + 1) * RD],
                                                   aux_ps[:, 1, t * CB + hd * RD:t * CB + (hd + 1) * RD],
                                                   ACT.Square, accum_out=ssum[:, 2 * t + hd:2 * t + hd + 1])
                ins.then_inc(ss_ready, 1)

            retention_tail(0, TAIL0, *first_tail())
            with act.Fori(1, R_TRIPS) as i:
                at = R0.over(i, R_N, R_W, R_B)
                bv, bq, bk, bg = r_blocks(i)
                step(at, bv)
                act.wait_ge(aux_filled[1], filled(i, 1, -1))
                take(at, bv, wslot(2), ACT.Copy)
                at = at.after(bv)
                step(at, bq)
                act.wait_ge(aux_filled[0], filled(i, 0, -2))
                take(at, bq, wslot(0), ACT.Copy)
                retention_tail(i, at.after(bq), bk, bg)

            def gates(G, first_hooks):
                step(G.start, G.first, first_hooks)
                take(G.start, G.first, wslot(0), ACT.Sigmoid)
                with act.Fori(0, G_TRIPS) as j:
                    at = G.loop.over(j, G_N, G_W, G_B)
                    bo, bgt = G.trip(j)
                    bo_at = at
                    step(at, bo)
                    at = at.after(bo)
                    step(at, bgt)
                    act.wait_ge(block_taken[bo_at.b.slot(2)], taken(bo_at.b))
                    take(at, bgt, wslot(0), ACT.Sigmoid)

            def take_gate_row(a, h, pair, filled):
                act.wait_ge(aux_filled[pair], filled)
                nc.scalar.activation(acc[:, a, h * CE:(h + 1) * CE], aux_ps[:, pair, :],
                                     ACT.Copy).then_inc(aux_freed[pair], 1)

            a0, a1 = AUX_GA
            gates(GA, {6: lambda: high_split(zT, 1, a1 + 1, 0),
                       7: lambda: high_split(zT, 0, a0 + 2, 4),
                       9: lambda: high_split(zT, 1, a1 + 2, 8),
                       10: lambda: high_split(zT, 0, a0 + 3, 12)})
            step(GA.last_at, GA.last)

            a0, a1 = AUX_S
            qfill = [a0 + 1, a1 + 1]

            def q_take(g):
                act.wait_ge(q_ready, g + 1)
                take(s_at[2 + g], s_blocks[2 + g], wslot(0), ACT.Copy)

            def take_kT(p):
                act.wait_ge(aux_filled[p], (a0, a1)[p] + 1)
                nc.scalar.activation(heads[:, p * 2 * CB:(p + 1) * 2 * CB], aux_ps[:, p, :],
                                     ACT.Copy).then_inc(aux_freed[p], 1)

            def take_qT(g):
                act.wait_ge(aux_filled[0], SW_FILL["q", g])
                nc.scalar.activation(work[:, 2, :], aux_ps[:, 0, :],
                                     ACT.Copy).then_inc(aux_freed[0], 1)

            def exps(g, t):
                act.wait_ge(max_ready, 2 * g + t + 1)
                if g:
                    act.wait_ge(aux_filled[t], SW_FILL["p", g - 1, t])
                for h in range(8):
                    ins = nc.scalar.activation(probs[:, t, h * P:(h + 1) * P], aux_ps[:, t, h * P:(h + 1) * P],
                                               ACT.Exp, bias=nmax[:, t, h:h + 1],
                                               accum_out=rowsum[:, t, h:h + 1])
                ins.then_inc(aux_freed[t], 1)
                nc.scalar.activation(esink[:, t, :], dsink[:, t, :], ACT.Exp).then_inc(exp_ready, 1)

            def take_pT(g, t):
                act.wait_ge(aux_filled[t], SW_FILL["p", g, t])
                if g:
                    act.wait_ge(o_high, 2 * g)
                nc.scalar.activation(probsT[:, t, :], aux_ps[:, t, :],
                                     ACT.Copy).then_inc(aux_freed[t], 1)

            def o_take(g, t):
                act.wait_ge(aux_filled[t], SW_FILL["o", g, t])
                nc.scalar.activation(zT[:, 0, 4 * g:4 * g + 4, t * P:(t + 1) * P],
                                     aux_ps[:, t, 0:CB].rearrange("p (k n) -> p k n", k=4),
                                     ACT.Copy).then_inc(o_high, 1)

            def take_pTs(g):
                take_pT(g, 0)
                take_pT(g, 1)

            def o_takes(g):
                o_take(g, 0)
                o_take(g, 1)

            step(s_at[0], s_blocks[0])
            act.wait_ge(aux_freed[1], AUX_GA[1])
            take(s_at[0], s_blocks[0], wslot(3), ACT.Copy)
            step(s_at[1], s_blocks[1])
            q = GA.last_at.b.slot(2)
            act.wait_ge(block_taken[q], taken(GA.last_at.b))
            take(s_at[1], s_blocks[1], wslot(0), ACT.Copy)
            step(s_at[2], s_blocks[2])
            take_kT(0)
            take_kT(1)
            q_take(0)
            for g in range(3):
                hooks = {}
                if g:
                    hooks = {4: lambda: exps(g - 1, 1), 8: lambda: take_pT(g - 1, 0),
                             9: lambda: take_pT(g - 1, 1), 10: lambda: o_takes(g - 1)}
                step(s_at[3 + g], s_blocks[3 + g], hooks)
                take_qT(g)
                q_take(g + 1)
                exps(g, 0)
            step(GB.first_at[0], GB.firsts[0],
                 {4: lambda: exps(2, 1), 8: lambda: take_pT(2, 0), 9: lambda: take_pT(2, 1),
                  10: lambda: o_takes(2)})
            take_qT(3)
            exps(3, 0)

            def first_gate():
                act.wait_ge(q_ready, 5)
                take(GB.first_at[0], GB.firsts[0], wslot(0), ACT.Sigmoid)

            step(GB.first_at[1], GB.firsts[1],
                 {4: lambda: exps(3, 1), 6: first_gate, 8: lambda: take_pT(3, 0), 9: lambda: take_pT(3, 1),
                  10: lambda: o_takes(3)})
            take(GB.first_at[1], GB.firsts[1], wslot(1), ACT.Sigmoid)
            with act.Fori(0, GB.TRIPS) as j:
                at = GB.loop.over(j, G_N, G_W, G_B)
                bo, bgt = GB.trip(j)
                step(at, bo)
                at = at.after(bo)
                step(at, bgt)
                act.wait_ge(merged, j + 1)
                take(at, bgt, work[:, bass.ds(j, 1), :].rearrange("p a (t n) -> p (a t) n", t=TT), ACT.Sigmoid)
            step(GB.last_at[0], GB.lasts[0])
            g0, g1 = AUX_GB
            step(GB.last_at[1], GB.lasts[1], {6: lambda: high_split(hT, 0, g0 + 1, 0),
                                              8: lambda: high_split(hT, 1, g1 + 1, 4),
                                              10: lambda: high_split(hT, 0, g0 + 2, 8)})
            def high_affine(k, filled):
                g, pair = k % 4, k % 2
                act.wait_ge(aux_filled[pair], filled)
                if k >= 6:
                    act.wait_ge(hT_ready, k - 1)
                for m in range(2, 4):
                    kt = 4 * g + m
                    ins = nc.scalar.activation(tmp[:, pair, m * SEQ:(m + 1) * SEQ],
                                               aux_ps[:, pair, m * SEQ:(m + 1) * SEQ], ACT.Identity,
                                               bias=modB[:, kt:kt + 1], scale=modA[:, kt:kt + 1])
                ins.then_inc(own_affine, 1)
                act.wait_ge(own_affine, k - 3)
                high_h(k, pair, filled)

            o0, o1 = AUX_O
            step(o_at[0], o_blocks[0], {6: lambda: high_split(hT, 1, o1 + 1, 12),
                                        8: lambda: take_gate_row(0, 0, 0, o0 + 1),
                                        9: lambda: take_gate_row(0, 1, 1, o1 + 2)})
            for j in range(4):
                if j:
                    step(o_at[j], o_blocks[j])
                act.wait_ge(x1_ready, j + 1)
                for t in range(TT):
                    ins = nc.scalar.activation(probs[:, t, 0:CB], res[:, t, j * CB:(j + 1) * CB], ACT.Square,
                                               accum_out=xsum[:, t, j:j + 1])
                ins.then_inc(ss_ready, 1)
            take_gate_row(1, 0, 0, o0 + 2)
            take_gate_row(1, 1, 1, o1 + 3)
            high_affine(4, AUX_F[0] - 1)
            high_affine(5, AUX_F[1] - 1)

            for p, part in enumerate(parts):
                def ffn_pair(at, j, k, T=None):
                    gate, up = part.pair(j)
                    hooks = {8: T} if T else {}
                    if isinstance(k, int) and k == 0:
                        hooks = {4: lambda: high_affine(6, AUX_F[0]), 5: lambda: high_affine(7, AUX_F[1])}
                    step(at, gate, hooks)
                    act.wait_ge(block_taken[1], taken(at.b + -1))
                    take(at, gate, wslot(0), ACT.Silu)
                    at = at.after(gate)
                    step(at, up)

                f1 = AUX_F[1] + 4 * p
                ffn_pair(part.start, 0, part.first)
                with act.Fori(1, part.pairs) as j:
                    ffn_pair(shifted(part.loop, j), j, j + part.first,
                             lambda: high_split(zT, 1, j + f1, j * 4 - 4))
                for m, (at_, blk) in enumerate(zip(part.out_at, part.outs)):
                    last = p == len(parts) - 1 and m == 3
                    hooks = {5: lambda: high_split(zT, 1, f1 + part.pairs, 4 * part.pairs - 4)} if m == 0 else {}
                    step(at_, blk, hooks, nxt=not last)

        @block.vector
        def _(dve):
            chain = [At(0)]

            def link(ins):
                ins.then_inc(dve_chain, 1)
                chain[0] = chain[0] + 1
                return ins

            def settle():
                dve.wait_ge(dve_chain, chain[0].value())

            def low(at, blk, k):
                n, w = at.n + blk.offset(k), at.w + k
                s, r = w.slot(SPL), n.slot(RAW)
                dve.wait_ge(high_ready, (w + 1).value())
                nc.vector.tensor_tensor(split[:, s, 1, :, :], raw[:, r, :].rearrange("p (k n) -> p k n", k=KC),
                                        split[:, s, 0, :, :].bitcast(F32), ALU.subtract).then_inc(chunk_done, 1)

            def ada(n, a, kt, half):
                r = n.slot(RAW)
                dve.wait_ge(raw_landed[r], (n + RAW).value(16, RAW))
                dve.wait_ge(chunk_done, (n + (-1)).value())
                dst = acc[:, a, half * CE:(half + 1) * CE]
                nc.vector.scalar_tensor_tensor(out=dst, in0=raw[:, r, :], scalar=vecs[:, 0, bass.ds(kt, 1)],
                                               in1=dst, op0=ALU.mult, op1=ALU.add).then_inc(chunk_done, 1)

            def step(at, blk, hooks=None, nxt=True):
                hooks = hooks or {}
                for k in range(AHEAD, blk.chunks + (AHEAD if nxt else 0)):
                    if k in hooks:
                        hooks[k]()
                    if k >= blk.chunks:
                        low(at.after(blk), FIRST, k - blk.chunks)
                        continue
                    low(at, blk, k)
                    for m, (a, _, kt, half) in enumerate(blk.ada_after(k)):
                        ada(at.n + (blk.offset(k) + 1 + m), a, kt, half)

            FIRST = Block("", 0)

            invf = inv_freq_sb
            dve.wait_ge(small_in[1], 32)
            link(nc.vector.tensor_copy(pos_f[:, :], pos_i[:, :]))
            settle()
            ang = angles
            turns, hi, lo_ = half_sin, turns_hi, turns_lo
            for t in range(TT):
                link(nc.vector.tensor_scalar(ang[:, t * P:(t + 1) * P], invf, pos_f[:, t:t + 1], None, ALU.mult))
            settle()
            link(nc.vector.tensor_scalar(turns, ang, 1.0 / _TP, ROUND, ALU.mult, ALU.add))
            settle()
            link(nc.vector.tensor_scalar(turns, turns, ROUND, None, ALU.subtract))
            settle()
            link(nc.vector.tensor_scalar(hi, turns, ROUND_HI, None, ALU.add))
            settle()
            link(nc.vector.tensor_scalar(hi, hi, ROUND_HI, None, ALU.subtract))
            settle()
            link(nc.vector.tensor_tensor(lo_, turns, hi, ALU.subtract))
            settle()
            for mult, by in ((hi, TP1), (lo_, TP1), (hi, TP2), (lo_, TP2), (turns, TP3)):
                link(nc.vector.scalar_tensor_tensor(out=ang, in0=mult, scalar=-by, in1=ang,
                                                    op0=ALU.mult, op1=ALU.add))
                settle()
            PI = 3.1415925
            nc.vector.tensor_scalar(ang, ang, PI, -PI, ALU.min, ALU.max).then_inc(ang_ready, 1)

            def mean_square(k, src, cols, width):
                nc.vector.tensor_scalar(msq[:, 0:cols], src, 1.0 / width, EPS,
                                        ALU.mult, ALU.add).then_inc(ms_ready, 1)

            dve.wait_ge(vecs_ready, 1)
            dve.wait_ge(aux_freed[0], 1)
            dve.wait_ge(bias_landed, 32)

            def take_mod(pair, filled, gain, kt=0, n=KT):
                dve.wait_ge(aux_filled[pair], filled)
                link(nc.vector.tensor_copy(modB[:, kt:kt + n], aux_ps[:, pair, 0:n]))
                link(nc.vector.scalar_tensor_tensor(out=modA[:, kt:kt + n], in0=aux_ps[:, pair, n:2 * n], scalar=1.0,
                                                    in1=vecs[:, gain, kt:kt + n], op0=ALU.add, op1=ALU.mult))
                settle()
                nc.vector.tensor_copy(den[:, 0, 0:1], modA[:, 0:1]).then_inc(aux_freed[pair], 1)

            def affine(k, pair, filled):
                g = k % 4
                dve.wait_ge(aux_filled[pair], filled)
                if k >= 2:
                    dve.wait_ge(hT_ready, k - 1)
                for m in range(2):
                    kt = 4 * g + m
                    ins = nc.vector.tensor_scalar(tmp[:, k % 2, m * SEQ:(m + 1) * SEQ],
                                                  aux_ps[:, pair, m * SEQ:(m + 1) * SEQ],
                                                  modA[:, kt:kt + 1], modB[:, kt:kt + 1], ALU.mult, ALU.add)
                ins.then_inc(aux_freed[pair], 1)

            def low_h(k):
                dve.wait_ge(hT_high, k + 1)
                g = k % 4
                nc.vector.tensor_tensor(hT[:, 1, 4 * g:4 * g + 4, :],
                                        tmp[:, k % 2, :].rearrange("p (k n) -> p k n", k=4),
                                        hT[:, 0, 4 * g:4 * g + 4, :].bitcast(F32),
                                        ALU.subtract).then_inc(hT_ready, 1)

            for n, (kind, g, k) in enumerate(STREAM):
                if (kind, g, k) == ("ada", 0, 12):
                    dve.wait_ge(ss_ready, 1)
                    mean_square(1, xsum[:, :, 0], TT, D)
                if (kind, k) == ("ada", Q_MOD) and g:
                    take_mod(1, g, 1, 4 * (g - 1), 4)
                if (kind, k) == ("w", 0):
                    if g == QUARTERS - 1:
                        take_mod(1, QUARTERS, 1, 4 * g, 4)
                    low_h(g)
                if kind == "w":
                    low(Place(n - k, 4 * g), FIRST, k)
                    continue
                dve.wait_ge(raw_landed[n % RAW], 16 * (n // RAW + 1))
                if k:
                    dve.wait_ge(chunk_done, n)
                dst = acc[:, :, g * CB:(g + 1) * CB]
                nc.vector.scalar_tensor_tensor(
                    out=dst, in0=raw[:, n % RAW, :].rearrange("p (s n) -> p s n", s=2),
                    scalar=vecs[:, 0, k:k + 1], in1=dst, op0=ALU.mult, op1=ALU.add).then_inc(chunk_done, 1)
            for k in range(AHEAD):
                low(TAIL0, FIRST, k)
            dve.wait_ge(sin_ready, 2)
            half_s = half_sin
            link(nc.vector.tensor_tensor(hi, half_s, half_s, ALU.mult))
            settle()
            link(nc.vector.tensor_scalar(cos_r[:, :, :], hi.rearrange("p (t n) -> p t n", t=TT), -2.0, 1.0,
                                         ALU.mult, ALU.add))
            settle()
            dve.wait_ge(bias_landed, 64)

            R_LINKS = 6
            a0, a1 = AUX_R

            def rope(slot, b):
                dve.wait_ge(block_taken[b.slot(2)], taken(b))
                xs = work[:, slot, :].rearrange("p (t h n) -> p t h n", t=TT, h=4)
                for m, table in enumerate((cos_r, sin_r)):
                    link(nc.vector.tensor_tensor(
                        tmp[:, m, :].rearrange("p (t h n) -> p t h n", t=TT, h=4), xs,
                        table[:, :, :].unsqueeze(2).to_broadcast([P, TT, 4, P]), ALU.mult))
                settle()
                v = [y.rearrange("p (t h n) -> p t h n", h=2, n=P)
                     for y in (work[:, slot, :], tmp[:, 0, :], tmp[:, 1, :])]
                link(nc.vector.tensor_tensor(v[0][:, :, 0, :], v[1][:, :, 0, :], v[2][:, :, 1, :], ALU.subtract))
                settle()
                nc.vector.tensor_tensor(v[0][:, :, 1, :], v[1][:, :, 1, :], v[2][:, :, 0, :],
                                        ALU.add).then_inc(roped, 1)

            def mask(i):
                dve.wait_ge(aux_filled[0], i * 2 + (a0 + 2))
                dve.wait_ge(decay_landed, i * 16 + 16)
                dve.wait_ge(aux_filled[1], i * 2 + a1)
                nc.vector.tensor_tensor(maskd[:, :, :],
                                        aux_ps[:, 0, :].rearrange("p (h n) -> p h n", h=2)[:, :, 0:3 * P],
                                        decay_sb[:, :, :], ALU.mult).then_inc(aux_freed[0], 1)

            def retention_tail(i, at, bk, bg):
                step(at, bk)
                rope(1, at.b)
                at = at.after(bk)
                step(at, bg, {9: lambda: mask(i)})
                dve.wait_ge(ss_ready, i + 2)
                mean_square(0, ssum[:, 0:4], 4, RD)
                dve.wait_ge(rstd_ready, i + 2)
                dve.wait_ge(block_taken[at.b.slot(2)], taken(at.b))
                for t in range(TT):
                    for hd in range(2):
                        c0 = t * CB + hd * RD
                        ins = nc.vector.scalar_tensor_tensor(
                            out=res[:, t, bass.ds(i * CB + hd * RD, RD)], in0=aux_ps[:, 1, c0:c0 + RD],
                            scalar=rstd[:, 2 * t + hd:2 * t + hd + 1], in1=work[:, 3, c0:c0 + RD],
                            op0=ALU.mult, op1=ALU.mult)
                ins.then_inc(aux_freed[1], 1)

            start = chain[0].fixed
            rope(0, Q0.b)
            retention_tail(0, TAIL0, *first_tail())
            assert chain[0].fixed == start + R_LINKS
            with dve.Fori(1, R_TRIPS) as i:
                chain[0] = At(start).over(i, R_LINKS)
                at = R0.over(i, R_N, R_W, R_B)
                bv, bq, bk, bg = r_blocks(i)
                step(at, bv)
                at = at.after(bv)
                step(at, bq)
                rope(0, at.b)
                retention_tail(i, at.after(bq), bk, bg)
            chain[0] = At(start + R_TRIPS * R_LINKS)

            def low_split(dst, k, pair, kt):
                dve.wait_ge(split_high, k)
                nc.vector.tensor_tensor(dst[:, 1, bass.ds(kt, 4), :],
                                        aux_ps[:, pair, :].rearrange("p (k n) -> p k n", k=4),
                                        dst[:, 0, bass.ds(kt, 4), :].bitcast(F32),
                                        ALU.subtract).then_inc(aux_freed[pair], 1)

            def own_take(at):
                dve.wait_ge(block_taken[at.b.slot(2)], taken(at.b))

            def merge(at, blk, j, k, slot=0):
                dve.wait_ge(w_used, (at.w + (blk.chunks + 1)).value())
                b = at.b + (-1 if k == 0 else -2)
                dve.wait_ge(block_taken[b.slot(2)], taken(b))
                q = at.b.slot(2)
                dst = res[:, :, bass.ds(j * CB, CB)]
                sg = (wslot(slot) if isinstance(slot, int) else
                      work[:, bass.ds(slot, 1), :].rearrange("p a (t n) -> p (a t) n", t=TT))
                if k == 0:
                    nc.vector.tensor_tensor(dst, gemm_ps[:, q, :, :], sg, ALU.mult).then_inc(block_taken[q], 1)
                    return
                t3 = tmp[:, 0, :].rearrange("p (t n) -> p t n", t=TT)
                nc.vector.tensor_tensor(t3, gemm_ps[:, q, :, :], sg, ALU.mult).then_inc(block_taken[q], 1)
                own_take(at)
                nc.vector.tensor_tensor(dst, dst, t3, ALU.add).then_inc(merged, 1)

            def gates(G, first_hooks, k, last_hooks=None):
                step(G.start, G.first, first_hooks)
                with dve.Fori(0, G_TRIPS) as j:
                    at = G.loop.over(j, G_N, G_W, G_B)
                    bo, bgt = G.trip(j)
                    step(at, bo)
                    merge(at, bo, j, k)
                    step(at.after(bo), bgt)
                step(G.last_at, G.last, last_hooks)
                merge(G.last_at, G.last, 3, k)

            gates(GA, {4: lambda: (take_mod(0, AUX_GA[0] + 1, 2), dve.wait_ge(bias_landed, 96)),
                       7: lambda: low_split(zT, 1, 1, 0),
                       8: lambda: low_split(zT, 2, 0, 4),
                       9: lambda: low_split(zT, 3, 1, 8),
                       10: lambda: low_split(zT, 4, 0, 12)}, 0)

            dve.wait_ge(small_in[2], 48)
            step4 = RD // HD
            for table, gi, scale in ((rope_q, 0, HD ** -0.5), (rope_k, 1, 1.0)):
                for kind, src in enumerate((cos_r, sin_r)):
                    for t in range(TT):
                        for hf in range(2):
                            o = table[:, kind, t, hf * 32:(hf + 1) * 32]
                            link(nc.vector.scalar_tensor_tensor(
                                out=o, in0=src[:, t, 0:P:step4], scalar=scale,
                                in1=gains[:, gi, hf * 32:(hf + 1) * 32], op0=ALU.mult, op1=ALU.mult))
            settle()

            def rms_begin(k):
                dve.wait_ge(q_squared, k + 1)
                link(nc.vector.tensor_reduce(ssum[:, 0:16], tmp[:, 1, :].rearrange("p (h n) -> p h n", n=HD),
                                             AXX, ALU.add))
                settle()
                mean_square(0, ssum[:, 0:16], 16, HD)

            def rms_rope(table):
                xs = work[:, 0, :].rearrange("p (t h n) -> p t h n", t=TT, h=8)
                for m in range(2):
                    link(nc.vector.tensor_tensor(
                        tmp[:, m, :].rearrange("p (t h n) -> p t h n", t=TT, h=8), xs,
                        table[:, m, :, :].unsqueeze(2).to_broadcast([P, TT, 8, HD]), ALU.mult))
                settle()
                v = [y.rearrange("p (t h n) -> p t h n", h=2, n=HD // 2)
                     for y in (work[:, 0, :], tmp[:, 0, :], tmp[:, 1, :])]
                link(nc.vector.tensor_tensor(v[0][:, :, 0, :], v[1][:, :, 0, :], v[2][:, :, 1, :], ALU.subtract))
                link(nc.vector.tensor_tensor(v[0][:, :, 1, :], v[1][:, :, 1, :], v[2][:, :, 0, :], ALU.add))
                settle()

            def rms_end(k):
                dve.wait_ge(rstd_ready, R_TRIPS + 2 + k)
                if k == 1:
                    dve.wait_ge(aux_filled[1], AUX_S[1] + 1)
                elif k:
                    dve.wait_ge(aux_filled[0], SW_FILL["q", k - 2])
                src = work[:, 0, :].rearrange("p (h n) -> p h n", n=HD)
                if k == 0:
                    dst = work[:, 1:3, :].rearrange("p a (h c n) -> p (a h) c n", c=2, n=HD)
                    for cpy in range(2):
                        ins = nc.vector.tensor_tensor(dst[:, :, cpy, :], src,
                                                      rstd[:, 0:16].unsqueeze(2).to_broadcast([P, 16, HD]), ALU.mult)
                else:
                    dst = work[:, 1, :].rearrange("p (h n) -> p h n", n=HD)
                    ins = nc.vector.tensor_tensor(dst, src, rstd[:, 0:16].unsqueeze(2).to_broadcast([P, 16, HD]),
                                                  ALU.mult)
                ins.then_inc(q_ready, 1)

            def maxima(g, t):
                dve.wait_ge(aux_filled[t], SW_FILL["l", g, t])
                L = aux_ps[:, t, :].rearrange("p (h j) -> p h j", h=8)
                if t == 0:
                    link(nc.vector.memset(L[0:CHUNK, :, CHUNK:P], NEG))
                    settle()
                link(nc.vector.tensor_reduce(smax[:, t, :], L, AXX, ALU.max))
                settle()
                sk = sink_b[:, 8 * g:8 * g + 8].rearrange("p (m e) -> p e m", e=2)
                top = smax[:, t, :].rearrange("p (e m) -> p e m", e=2)
                link(nc.vector.tensor_tensor(top, top, sk, ALU.max))
                settle()
                link(nc.vector.tensor_scalar(nmax[:, t, :], smax[:, t, :], -1.0, None, ALU.mult))
                nc.vector.tensor_tensor(dsink[:, t, :].rearrange("p (e m) -> p e m", e=2), sk, top, ALU.subtract).then_inc(max_ready, 1)

            def denominators(g, t):
                dve.wait_ge(exp_ready, 2 * g + t + 1)
                link(nc.vector.tensor_tensor(den[:, t, :], rowsum[:, t, :], esink[:, t, :], ALU.add))
                settle()
                nc.vector.reciprocal(rden[:, t, :], den[:, t, :]).then_inc(rden_ready, 1)

            def o_low(g, t):
                dve.wait_ge(o_high, 2 * g + t + 1)
                nc.vector.tensor_tensor(zT[:, 1, 4 * g:4 * g + 4, t * P:(t + 1) * P],
                                        aux_ps[:, t, 0:CB].rearrange("p (k n) -> p k n", k=4),
                                        zT[:, 0, 4 * g:4 * g + 4, t * P:(t + 1) * P].bitcast(F32),
                                        ALU.subtract).then_inc(aux_freed[t], 1)

            step(s_at[0], s_blocks[0])
            step(s_at[1], s_blocks[1])
            rms_begin(0)
            step(s_at[2], s_blocks[2], {4: lambda: rms_rope(rope_k), 5: lambda: rms_end(0)})
            rms_begin(1)
            for g in range(3):
                hooks = {4: lambda: rms_rope(rope_q), 5: lambda: rms_end(g + 1)}
                if g:
                    hooks[4] = lambda: (rms_rope(rope_q), denominators(g - 1, 1))
                    hooks[10] = lambda: (o_low(g - 1, 0), o_low(g - 1, 1))
                step(s_at[3 + g], s_blocks[3 + g], hooks)
                maxima(g, 0)
                maxima(g, 1)
                rms_begin(g + 2)
                denominators(g, 0)
            step(GB.first_at[0], GB.firsts[0],
                 {4: lambda: (rms_rope(rope_q), denominators(2, 1)), 5: lambda: rms_end(4),
                  10: lambda: (o_low(2, 0), o_low(2, 1))})
            maxima(3, 0)
            maxima(3, 1)
            denominators(3, 0)
            step(GB.first_at[1], GB.firsts[1],
                 {4: lambda: denominators(3, 1), 10: lambda: (o_low(3, 0), o_low(3, 1))})
            with dve.Fori(0, GB.TRIPS) as j:
                at = GB.loop.over(j, G_N, G_W, G_B)
                bo, bgt = GB.trip(j)
                step(at, bo)
                merge(at, bo, j, 4, j)
                step(at.after(bo), bgt)
            step(GB.last_at[0], GB.lasts[0])
            merge(GB.last_at[0], GB.lasts[0], 2, 4, 0)
            step(GB.last_at[1], GB.lasts[1], {7: lambda: low_split(hT, 5, 0, 0), 9: lambda: low_split(hT, 6, 1, 4),
                                              10: lambda: low_split(hT, 7, 0, 8)})
            merge(GB.last_at[1], GB.lasts[1], 3, 4, 1)

            def gate_rows(k):
                dve.wait_ge(aux_freed[0], AUX_O[0] + k)
                dve.wait_ge(aux_freed[1], AUX_O[1] + 1 + k)

            for j in range(4):
                step(o_at[j], o_blocks[j], {6: lambda: low_split(hT, 8, 1, 12)} if j == 0 else {})
                dve.wait_ge(w_used, (o_at[j].w + (NCH + 1)).value())
                if j == 0:
                    gate_rows(1)
                q = o_at[j].b.slot(2)
                t3 = tmp[:, 0, :].rearrange("p (t n) -> p t n", t=TT)
                nc.vector.tensor_tensor(
                    t3, gemm_ps[:, q, :, :],
                    acc[:, 0, j * CB:(j + 1) * CB].unsqueeze(1).to_broadcast([P, TT, CB]),
                    ALU.mult).then_inc(block_taken[q], 1)
                own_take(o_at[j])
                dve.wait_ge(x_again[j % 2], 16 * (j // 2 + 1))
                nc.vector.tensor_tensor(res[:, :, j * CB:(j + 1) * CB], t3,
                                        work[:, j % 2, :].rearrange("p (t n) -> p t n", t=TT),
                                        ALU.add).then_inc(x1_ready, 1)
            dve.wait_ge(ss_ready, 1 + R_TRIPS + 4)
            link(nc.vector.tensor_reduce(ssum[:, 0:TT], xsum[:, :, :], AXX, ALU.add))
            settle()
            mean_square(0, ssum[:, 0:TT], TT, D)
            dve.wait_ge(rstd_ready, R_TRIPS + 7)
            w4 = work[:, :, :].rearrange("p a n -> p (a n)").rearrange("p (t n) -> p t n", t=TT)
            for g in range(4):
                for t in range(TT):
                    c = slice(4 * g * P, 4 * (g + 1) * P)
                    ins = nc.vector.tensor_scalar(w4[:, t, c], res[:, t, c], rstd[:, t:t + 1], None, ALU.mult)
                ins.then_inc(norm_ready, 1)
                if g == 1:
                    affine(4, 0, AUX_F[0] - 1)
                    low_h(4)
            f0, f1 = AUX_F
            affine(5, 1, f1 - 1)
            low_h(5)

            def glu(at, up, k):
                dve.wait_ge(w_used, (at.w + (up.chunks + 1)).value())
                dve.wait_ge(block_taken[(at.b + -1).slot(2)], taken(at.b + -1))
                q = at.b.slot(2)
                dve.wait_ge(aux_filled[1], k + (f1 - 1))
                nc.vector.tensor_tensor(work[:, 1, :].rearrange("p (t n) -> p t n", t=TT), gemm_ps[:, q, :, :],
                                        work[:, 0, :].rearrange("p (t n) -> p t n", t=TT),
                                        ALU.mult).then_inc(block_taken[q], 1)

            splits = 8
            for p, part in enumerate(parts):
                def ffn_pair(at, j, k, T=None):
                    gate, up = part.pair(j)
                    hooks = {9: T} if T else {}
                    if isinstance(k, int) and k == 0:
                        hooks = {4: lambda: (affine(6, 0, f0), low_h(6)), 5: lambda: (affine(7, 1, f1), low_h(7))}
                    step(at, gate, hooks)
                    at = at.after(gate)
                    step(at, up)
                    glu(at, up, k + 1)

                ffn_pair(part.start, 0, part.first)
                with dve.Fori(1, part.pairs) as j:
                    ffn_pair(shifted(part.loop, j), j, j + part.first,
                             lambda: low_split(zT, j + splits, 1, j * 4 - 4))
                splits += part.pairs
                for m, (at_, blk) in enumerate(zip(part.out_at, part.outs)):
                    last = p == len(parts) - 1
                    hooks = {6: lambda: low_split(zT, splits, 1, 4 * part.pairs - 4)} if m == 0 else {}
                    step(at_, blk, hooks, nxt=not (last and m == 3))
                    dve.wait_ge(w_used, (at_.w + (blk.chunks + 1)).value())
                    if p == 0 and m == 0:
                        gate_rows(2)
                    q = at_.b.slot(2)
                    for ts in ([slice(0, 1), slice(1, 2)] if last and m == 3 else [slice(0, TT)]):
                        t3 = tmp[:, 0, :].rearrange("p (t n) -> p t n", t=TT)[:, ts, :]
                        ins = nc.vector.tensor_tensor(
                            t3, gemm_ps[:, q, ts, :],
                            acc[:, 1, m * CB:(m + 1) * CB].unsqueeze(1).to_broadcast([P, ts.stop - ts.start, CB]),
                            ALU.mult)
                        if ts.stop == TT:
                            ins.then_inc(block_taken[q], 1)
                            own_take(at_)
                        else:
                            link(ins)
                        settle()
                        dst = res[:, ts, m * CB:(m + 1) * CB]
                        ins = nc.vector.tensor_tensor(dst, dst, t3, ALU.add)
                        if last:
                            ins.then_inc(out_ready, 1)
                        else:
                            link(ins)

        @block.tensor
        def _(pe):
            def products(q, src, s, kt0, last_kt):
                for m in range(KC):
                    kt = kt0 + m
                    for t in range(TT):
                        for a, b in ((0, 0), (0, 1), (1, 0)):
                            ins = nc.tensor.matmul(gemm_ps[:, q, t, :], src[:, a, kt, t * P:(t + 1) * P],
                                                   split[:, s, b, m, :], start=kt == 0 and a == 0 and b == 0,
                                                   stop=kt == last_kt and a == 1)
                ins.then_inc(w_used, 1)

            def gemm(at, blk, src, hooks=None):
                hooks = hooks or {}
                q = at.b.slot(2)
                pe.wait_ge(block_taken[q], taken(at.b + -2))
                last_kt = blk.chunks * KC - 1
                for k in range(blk.chunks):
                    if k in hooks:
                        hooks[k]()
                    pe.wait_ge(chunk_done, (at.n + (blk.offset(k) + 1)).value())
                    products(q, src, (at.w + k).slot(SPL), KC * k, last_kt)
                if blk.chunks in hooks:
                    hooks[blk.chunks]()

            uses = [At(0), At(0)]

            def aux(pair):
                if uses[pair].loops or uses[pair].fixed:
                    pe.wait_ge(aux_freed[pair], uses[pair].value())
                uses[pair] = uses[pair] + 1

            def emptied(pair):
                pe.wait_ge(aux_freed[pair], uses[pair].value())

            def enter(reg, per_trip, first=0):
                before = [u.fixed for u in uses]
                for p in range(2):
                    uses[p] = At(before[p] - first * per_trip[p]).over(reg, per_trip[p])
                return before

            def leave(before, per_trip, trips):
                for p in range(2):
                    uses[p] = At(before[p] + per_trip[p] * trips)

            def transpose_group(pair, src):
                aux(pair)
                for m in range(4):
                    for t in range(TT):
                        ins = nc.tensor.transpose(aux_ps[:, pair, (m * TT + t) * P:(m * TT + t + 1) * P],
                                                  src[:, t, m * P:(m + 1) * P], ident[:, :])
                ins.then_inc(aux_filled[pair], 1)

            def mod_columns(pair, kt=0, n=KT):
                aux(pair)
                for s in range(2):
                    for m in range(n):
                        ins = nc.tensor.matmul(aux_ps[:, pair, s * n + m:s * n + m + 1],
                                               acc[:, s, (kt + m) * P:(kt + m + 1) * P], ones[:, 0:1],
                                               start=True, stop=True)
                ins.then_inc(aux_filled[pair], 1)

            def gate_rows(pair, a, h):
                aux(pair)
                for m in range(2):
                    c0 = h * CE + m * CB
                    ins = nc.tensor.matmul(aux_ps[:, pair, m * CB:(m + 1) * CB], ones[:, :], acc[:, a, c0:c0 + CB],
                                           start=True, stop=True)
                ins.then_inc(aux_filled[pair], 1)

            pe.wait_ge(consts_ready, 4)
            pe.wait_ge(small_in[0], 48)
            aux(0)
            nc.tensor.transpose(aux_ps[:, 0, 0:P], tmp[:, 0, 0:P], ident[:, :]).then_inc(aux_filled[0], 1)
            nc.tensor.transpose(aux_ps[:, 1, 0:P], ident[:, :], ident[:, :]).then_inc(w_used, 1)
            pe.wait_ge(w_used, 1)
            for g in range(QUARTERS):
                if g == 0:
                    pe.wait_ge(norm_ready, 1)
                transpose_group(0, res[:, :, 4 * g * P:4 * (g + 1) * P])
                pe.wait_ge(chunk_done, STREAM.index(("ada", g, KT - 1)) + 1)
                mod_columns(1, 4 * g, 4)
                pe.wait_ge(hT_ready, g + 1)
                for m in range(2):
                    if g == 0:
                        pe.wait_ge(block_taken[m], taken(At(m - 2)))
                    for c in range(2):
                        k = 2 * m + c
                        pe.wait_ge(chunk_done, STREAM.index(("w", g, k)) + 1)
                        products(m, hT, (4 * g + k) % SPL, 4 * g + KC * c, KT - 1)

            def heads_to_T(i, slot, pair, k):
                pe.wait_ge(roped, i * 2 + (k + 1))
                aux(pair)
                for f in range(4):
                    for t in range(TT):
                        ins = nc.tensor.transpose(aux_ps[:, pair, (f * TT + t) * P:(f * TT + t + 1) * P],
                                                  work[:, slot, t * CB + f * P:t * CB + (f + 1) * P], ident[:, :])
                ins.then_inc(aux_filled[pair], 1)

            def scores():
                emptied(1)
                aux(0)
                qT = heads[:, 0:2 * CB].rearrange("p (h f n) -> p h f n", h=2, f=2)
                kT = heads[:, 2 * CB:4 * CB].rearrange("p (h f n) -> p h f n", h=2, f=2)
                for hd in range(2):
                    for c0, k0, q0, width in ((0, 0, 0, SEQ), (SEQ, P, P, P)):
                        for f in range(2):
                            ins = nc.tensor.matmul(aux_ps[:, 0, hd * CB + c0:hd * CB + c0 + width],
                                                   kT[:, hd, f, k0:k0 + P], qT[:, hd, f, q0:q0 + width],
                                                   start=f == 0, stop=f == 1)
                ins.then_inc(aux_filled[0], 1)

            def outputs(v_b):
                emptied(0)
                pe.wait_ge(block_taken[v_b.slot(2)], taken(v_b))
                aux(1)
                for t in range(TT):
                    for hd in range(2):
                        o = aux_ps[:, 1, t * CB + hd * RD:t * CB + (hd + 1) * RD]
                        for kt in range(t + 1):
                            s0 = t * P if kt == 0 else 2 * P
                            ins = nc.tensor.matmul(o, maskd[:, hd, s0:s0 + P],
                                                   work[:, 2, kt * CB + hd * RD:kt * CB + (hd + 1) * RD],
                                                   start=kt == 0, stop=kt == t)
                ins.then_inc(aux_filled[1], 1)

            def retention_tail(i, at, bk, bg, v_b):
                gemm(at, bk, hT, {6: lambda: heads_to_T(i, 0, 0, 0)})
                gemm(at.after(bk), bg, hT, {3: lambda: heads_to_T(i, 1, 1, 1), 5: scores,
                                            8: lambda: outputs(v_b)})

            retention_tail(0, TAIL0, *first_tail(), At(0))
            with pe.Fori(1, R_TRIPS) as i:
                before = enter(i, (2, 2), 1)
                at = R0.over(i, R_N, R_W, R_B)
                bv, bq, bk, bg = r_blocks(i)
                gemm(at, bv, hT)
                gemm(at.after(bv), bq, hT)
                retention_tail(i, at.after(bv).after(bq), bk, bg, at.b)
            leave(before, (2, 2), R_TRIPS - 1)

            def split_group(pair, src, kt):
                transpose_group(pair, src[:, :, kt * P:(kt + 4) * P])

            def gates_z(G, first_hooks, done, last_hooks=None):
                gemm(G.start, G.first, hT, first_hooks)
                done()
                with pe.Fori(0, G_TRIPS) as j:
                    at = G.loop.over(j, G_N, G_W, G_B)
                    bo, bgt = G.trip(j)
                    gemm(at, bo, zT)
                    gemm(at.after(bo), bgt, hT)
                gemm(G.last_at, G.last, zT, last_hooks)

            def first_y():
                emptied(1)

            gates_z(GA, {0: lambda: mod_columns(0), 2: lambda: (first_y(), split_group(1, res, 0)),
                         3: lambda: split_group(0, res, 4),
                         5: lambda: split_group(1, res, 8), 6: lambda: split_group(0, res, 12)},
                    lambda: (emptied(0), emptied(1)))

            gemm(s_at[0], s_blocks[0], hT)
            gemm(s_at[1], s_blocks[1], hT)

            def keys_to_T():
                pe.wait_ge(q_ready, 1)
                kd = work[:, 1:3, :].rearrange("p t n -> p (t n)")
                for p in range(2):
                    aux(p)
                    for kv in range(4):
                        for t in range(TT):
                            c0 = t * 2 * CB + (4 * p + kv) * 2 * HD
                            ins = nc.tensor.transpose(aux_ps[:, p, (kv * TT + t) * P:(kv * TT + t + 1) * P],
                                                      kd[:, c0:c0 + P], ident[:, :])
                    ins.then_inc(aux_filled[p], 1)

            gemm(s_at[2], s_blocks[2], hT, {7: keys_to_T})
            kT = heads[:, :].rearrange("p (h n) -> p h n", n=SEQ)
            qT = work[:, 2, :].rearrange("p (h n) -> p h n", n=SEQ)

            def queries_to_T(g):
                pe.wait_ge(q_ready, g + 2)
                aux(0)
                for f in range(4):
                    for t in range(TT):
                        ins = nc.tensor.transpose(aux_ps[:, 0, (f * TT + t) * P:(f * TT + t + 1) * P],
                                                  work[:, 1, t * CB + f * P:t * CB + (f + 1) * P], ident[:, :])
                ins.then_inc(aux_filled[0], 1)

            def logits(g):
                emptied(0)
                emptied(1)
                for t in range(TT):
                    aux(t)
                    L = aux_ps[:, t, :].rearrange("p (h j) -> p h j", h=8)
                    for h in range(8):
                        s = h % 2 * HD
                        kv = 2 * g + h // 4
                        for par in range(2):
                            q0 = t * P + par * CHUNK
                            lhsT = qT[s:s + HD, h // 2, q0:q0 + CHUNK]
                            o = L[par * CHUNK:(par + 1) * CHUNK, h % 2 * 4 + h // 2, :]
                            if par == 1:
                                keys = ((0, t * P, P),)
                            elif t == 1:
                                keys = ((0, P, CHUNK), (CHUNK, CHUNK, CHUNK))
                            else:
                                keys = ((0, 0, CHUNK),)
                            for c0, k0, width in keys:
                                ins = nc.tensor.matmul(o[:, c0:c0 + width], lhsT, kT[s:s + HD, kv, k0:k0 + width],
                                                       start=True, stop=True)
                    ins.then_inc(aux_filled[t], 1)

            def probs_to_T(g, t):
                pe.wait_ge(probs_ready, 2 * g + t + 1)
                aux(t)
                for h in range(8):
                    ins = nc.tensor.transpose(aux_ps[:, t, h * P:(h + 1) * P], probs[:, t, h * P:(h + 1) * P],
                                              ident[:, :])
                ins.then_inc(aux_filled[t], 1)

            def attend(g, t):
                pe.wait_ge(vmix_ready, 2)
                aux(t)
                pT = probsT[:, t, :].rearrange("p (h n) -> p h n", h=8)
                o = aux_ps[:, t, 0:CB].rearrange("p (k n) -> p k n", k=4)
                for par in range(2):
                    for kvl in range(2):
                        v0 = (2 * g + kvl) * HD
                        if par == 1:
                            v = work[:, 3, t * CB + v0:t * CB + v0 + HD]
                        elif t == 1:
                            v = vmix[:, v0:v0 + HD]
                        else:
                            v = work[0:CHUNK, 3, v0:v0 + HD]
                        rows = CHUNK if (t, par) == (0, 0) else P
                        for e in range(2):
                            ins = nc.tensor.matmul(
                                o[e * HD:(e + 1) * HD, 2 * kvl:2 * kvl + 2, par * CHUNK:(par + 1) * CHUNK], v,
                                pT[0:rows, 4 * e + 2 * kvl:4 * e + 2 * kvl + 2, par * CHUNK:(par + 1) * CHUNK],
                                start=True, stop=True)
                ins.then_inc(aux_filled[t], 1)

            def attention(g):
                return {4: lambda: probs_to_T(g, 0), 5: lambda: probs_to_T(g, 1),
                        6: lambda: (attend(g, 0), attend(g, 1))}

            for g in range(3):
                hooks = attention(g - 1) if g else {}
                hooks.update({7: lambda: queries_to_T(g), 8: lambda: logits(g)})
                gemm(s_at[3 + g], s_blocks[3 + g], hT, hooks)
            gemm(GB.first_at[0], GB.firsts[0], hT,
                 {**attention(2), 7: lambda: queries_to_T(3), 8: lambda: logits(3)})
            gemm(GB.first_at[1], GB.firsts[1], hT, attention(3))
            emptied(0)
            emptied(1)
            with pe.Fori(0, GB.TRIPS) as j:
                at = GB.loop.over(j, G_N, G_W, G_B)
                bo, bgt = GB.trip(j)
                gemm(at, bo, zT)
                gemm(at.after(bo), bgt, hT)
            gemm(GB.last_at[0], GB.lasts[0], zT)
            gemm(GB.last_at[1], GB.lasts[1], zT,
                    {2: lambda: (pe.wait_ge(merged, 3), split_group(0, res, 0)),
                     4: lambda: split_group(1, res, 4),
                     6: lambda: split_group(0, res, 8)})

            def last_merged():
                pe.wait_ge(merged, 4)
                split_group(1, res, 12)

            emptied(0)
            emptied(1)
            gemm(o_at[0], o_blocks[0], hT, {2: last_merged,
                                            4: lambda: gate_rows(0, 0, 0),
                                            5: lambda: gate_rows(1, 0, 1)})
            gemm(o_at[1], o_blocks[1], hT)
            gemm(o_at[2], o_blocks[2], hT)
            gemm(o_at[3], o_blocks[3], hT)
            w4 = work[:, :, :].rearrange("p a n -> p (a n)").rearrange("p (t n) -> p t n", t=TT)

            def h2_group(g):
                pe.wait_ge(norm_ready, g + 2)
                split_group(g % 2, w4, 4 * g)

            gate_rows(0, 1, 0)
            gate_rows(1, 1, 1)
            h2_group(0)
            h2_group(1)
            h2_hooks = {0: lambda: pe.wait_ge(hT_ready, 5), 1: lambda: h2_group(2),
                        2: lambda: (pe.wait_ge(hT_ready, 6), h2_group(3)),
                        4: lambda: pe.wait_ge(hT_ready, 7), 6: lambda: pe.wait_ge(hT_ready, 8)}

            act3 = work[:, 1, :].rearrange("p (t n) -> p t n", t=TT)
            for p, part in enumerate(parts):
                gate, up = part.pair(0)
                gemm(part.start, gate, hT, h2_hooks if p == 0 else {})
                gemm(part.start.after(gate), up, hT)
                with pe.Fori(1, part.pairs) as j:
                    before = enter(j, (0, 1), 1)
                    at = shifted(part.loop, j)
                    gate, up = part.pair(j)

                    def group():
                        pe.wait_ge(block_taken[1], taken(at.b + -1))
                        transpose_group(1, act3)

                    gemm(at, gate, hT, {4: group})
                    gemm(at.after(gate), up, hT)
                leave(before, (0, 1), part.pairs - 1)

                def last_group():
                    pe.wait_ge(block_taken[1], taken(part.out_at[0].b + -1))
                    transpose_group(1, act3)

                for m, (at_, blk) in enumerate(zip(part.out_at, part.outs)):
                    tail = blk.chunks - 2
                    hooks = {0: lambda: emptied(1), 1: last_group, tail: lambda: emptied(1)} if m == 0 else {}
                    gemm(at_, blk, zT, hooks)


def _constants():
    inv_freq = (THETA ** (-np.arange(0, RD, 2) / RD)).astype(np.float32)[None, :]
    lg = np.log1p(-np.exp2(-5.0 - np.arange(RH)))
    i = np.arange(SEQ)
    seen = (i[:, None] // CHUNK) <= (i[None, :] // CHUNK)
    d = np.exp(lg[:, None, None] * np.abs(i[:, None] - i[None, :])) * seen * RD ** -0.5
    decay = np.concatenate([d[:, :P, :], d[:, P:, P:]], axis=2).transpose(1, 0, 2)
    return inv_freq, np.ascontiguousarray(decay.astype(np.float32))


_INS = ["x", "c", "positions", "w_ada", "b_ada", "norm_mix_gain", "w_in", "q_norm_gain", "k_norm_gain",
        "sinks", "w_ret_out", "w_swa_out", "w_o", "norm_ffn_gain", "w_ffn_in", "w_ffn_out"]


def kernel(**inputs):
    import concourse.bacc as bacc
    from concourse.bass_utils import run_bass_kernel_spmd

    nc = bacc.Bacc("TRN2", target_bir_lowering=False, num_devices=1, dynamic_dma_scratch_size=2048)
    inv_freq, decay = _constants()
    arrays, args = {}, []
    given = [(name, np.ascontiguousarray(inputs[name])) for name in _INS]
    for name, a in given + [("inv_freq", inv_freq), ("decay", decay)]:
        arrays[f"in_{name}"] = a
        args.append(nc.dram_tensor(f"in_{name}", a.shape, mybir.dt.from_np(a.dtype), kind="ExternalInput").ap())
    out = nc.dram_tensor("out", (1, SEQ, D), F32, kind="ExternalOutput").ap()
    hybrid_block_kernel(nc, *args, out)
    r = run_bass_kernel_spmd(nc, [arrays], core_ids=[0])
    return r.results[0]["out"]
```
